# Optimizing a Trainium2 kernel written in Bass

```python
import math
import jax, jax.numpy as jnp
from jax import lax
import numpy as np

D_MODEL = 1024
BATCH = 1
SEQ = 512
DEPTH = 2

N_MIXERS = 2
CONV_WIDTH = 31
N_HEADS = 16
N_KV_HEADS = 2
HEAD_DIM = 64
GROUP = N_HEADS // N_KV_HEADS
WINDOW = 128
BLOCK = WINDOW
QKV_DIM = (N_HEADS + 2 * N_KV_HEADS) * HEAD_DIM
ATTN_DIM = N_HEADS * HEAD_DIM
D_FF = 4 * D_MODEL
REL_BUCKETS = 32
REL_MAX_DIST = 128
NORM_EPS = 1e-6
N_CONV_LAYERS = (DEPTH + 1) // 2
N_ATTN_LAYERS = DEPTH // 2
NEG_INF = -1e30

kernel_name = "hybrid_conformer_conv_swa_sink_trunk"

def rms_norm(x, g):
    xf = x.astype(jnp.float32)
    y = xf * lax.rsqrt(jnp.mean(xf * xf, axis=-1, keepdims=True) + NORM_EPS)
    return (y * g.astype(jnp.float32)).astype(x.dtype)

def layer_norm(x, g, b):
    xf = x.astype(jnp.float32)
    mu = jnp.mean(xf, axis=-1, keepdims=True)
    xc = xf - mu
    y = xc * lax.rsqrt(jnp.mean(xc * xc, axis=-1, keepdims=True) + NORM_EPS)
    return (y * g.astype(jnp.float32) + b.astype(jnp.float32)).astype(x.dtype)

def t5_causal_bucket(dist):
    n = np.maximum(dist, 0)
    max_exact = REL_BUCKETS // 2
    large = max_exact + (np.log(np.maximum(n, 1).astype(np.float32) / max_exact)
                         / math.log(REL_MAX_DIST / max_exact)
                         * (REL_BUCKETS - max_exact)).astype(np.int32)
    large = np.minimum(large, REL_BUCKETS - 1)
    return np.where(n < max_exact, n, large).astype(np.int32)

def conformer_conv(x, norm_g, w_in, b_in, dw, dw_b, ln_g, ln_b, w_out, b_out):
    h = rms_norm(x, norm_g)
    u = h @ w_in + b_in
    a, gate = jnp.split(u, 2, axis=-1)
    u = a * jax.nn.sigmoid(gate)
    u = lax.conv_general_dilated(
        u, dw[:, None, :].astype(u.dtype), window_strides=(1,),
        padding=[(CONV_WIDTH - 1, 0)],
        dimension_numbers=("NWC", "WIO", "NWC"),
        feature_group_count=D_MODEL) + dw_b
    u = jax.nn.silu(layer_norm(u, ln_g, ln_b))
    return u @ w_out + b_out

def swa_sink_attention(x, norm_g, w_qkv, b_qkv, q_g, k_g, sinks, w_o, b_o, rel_bias):
    B, S, _ = x.shape
    nb = S // BLOCK
    h = rms_norm(x, norm_g)
    qkv = h @ w_qkv + b_qkv
    q, k, v = jnp.split(qkv, [ATTN_DIM, ATTN_DIM + N_KV_HEADS * HEAD_DIM], axis=-1)
    q = rms_norm(q.reshape(B, S, N_HEADS, HEAD_DIM), q_g)
    k = rms_norm(k.reshape(B, S, N_KV_HEADS, HEAD_DIM), k_g)
    v = v.reshape(B, S, N_KV_HEADS, HEAD_DIM)

    qb = q.reshape(B, nb, BLOCK, N_KV_HEADS, GROUP, HEAD_DIM)

    def band(t):
        tp = jnp.pad(t, ((0, 0), (BLOCK, 0), (0, 0), (0, 0)))
        tb = tp.reshape(B, nb + 1, BLOCK, N_KV_HEADS, HEAD_DIM)
        return jnp.concatenate([tb[:, :-1], tb[:, 1:]], axis=2)

    kband, vband = band(k), band(v)

    q_loc = np.arange(BLOCK)[:, None]
    k_loc = np.arange(2 * BLOCK)[None, :]
    dist = q_loc + BLOCK - k_loc
    in_window = (dist >= 0) & (dist < WINDOW)
    k_abs = (np.arange(nb)[:, None, None] - 1) * BLOCK + k_loc[None]
    mask = jnp.asarray(in_window[None] & (k_abs >= 0))
    bias = rel_bias[jnp.asarray(t5_causal_bucket(dist))]
    bias = jnp.transpose(bias, (2, 0, 1)).reshape(N_KV_HEADS, GROUP, BLOCK, 2 * BLOCK)

    scale = 1.0 / math.sqrt(HEAD_DIM)
    logits = jnp.einsum("bnqkgd,bnskd->bnkgqs", qb, kband).astype(jnp.float32) * scale
    logits = logits + bias.astype(jnp.float32)[None, None]
    logits = jnp.where(mask[None, :, None, None], logits, NEG_INF)
    sink_col = jnp.broadcast_to(
        sinks.astype(jnp.float32).reshape(1, 1, N_KV_HEADS, GROUP, 1, 1),
        logits.shape[:-1] + (1,))
    probs = jax.nn.softmax(jnp.concatenate([logits, sink_col], axis=-1), axis=-1)[..., :-1]
    out = jnp.einsum("bnkgqs,bnskd->bnqkgd", probs.astype(vband.dtype), vband)
    out = out.reshape(B, S, ATTN_DIM)
    return out @ w_o + b_o

def sq_relu_mlp(x, norm_g, w_up, w_down):
    h = rms_norm(x, norm_g)
    return jnp.square(jax.nn.relu(h @ w_up)) @ w_down

def setup_inputs(seed: int = 0) -> dict:
    key = jax.random.key(seed)
    ks = iter(jax.random.split(key, 32))
    f32 = jnp.float32

    def nrm(shape, scale):
        return jax.random.normal(next(ks), shape, f32) * scale

    NC, NA = N_CONV_LAYERS, N_ATTN_LAYERS
    return {
        "x": nrm((BATCH, SEQ, D_MODEL), 1.0),
        "conv_norm_g": 1.0 + nrm((NC, D_MODEL), 0.02),
        "conv_w_in": nrm((NC, D_MODEL, 2 * D_MODEL), D_MODEL ** -0.5),
        "conv_b_in": nrm((NC, 2 * D_MODEL), 0.02),
        "conv_dw": nrm((NC, CONV_WIDTH, D_MODEL), CONV_WIDTH ** -0.5),
        "conv_dw_b": nrm((NC, D_MODEL), 0.02),
        "conv_ln_g": 1.0 + nrm((NC, D_MODEL), 0.02),
        "conv_ln_b": nrm((NC, D_MODEL), 0.02),
        "conv_w_out": nrm((NC, D_MODEL, D_MODEL), D_MODEL ** -0.5),
        "conv_b_out": nrm((NC, D_MODEL), 0.02),
        "attn_norm_g": 1.0 + nrm((NA, D_MODEL), 0.02),
        "w_qkv": nrm((NA, D_MODEL, QKV_DIM), D_MODEL ** -0.5),
        "b_qkv": nrm((NA, QKV_DIM), 0.02),
        "q_norm_g": 1.0 + nrm((NA, HEAD_DIM), 0.02),
        "k_norm_g": 1.0 + nrm((NA, HEAD_DIM), 0.02),
        "sinks": nrm((NA, N_HEADS), 0.5),
        "w_o": nrm((NA, ATTN_DIM, D_MODEL), ATTN_DIM ** -0.5),
        "b_o": nrm((NA, D_MODEL), 0.02),
        "rel_bias": nrm((REL_BUCKETS, N_HEADS), 0.5),
        "mlp_norm_g": 1.0 + nrm((DEPTH, D_MODEL), 0.02),
        "w_up": nrm((DEPTH, D_MODEL, D_FF), D_MODEL ** -0.5),
        "w_down": nrm((DEPTH, D_FF, D_MODEL), D_FF ** -0.5),
    }

def reference(x, conv_norm_g, conv_w_in, conv_b_in, conv_dw, conv_dw_b, conv_ln_g,
              conv_ln_b, conv_w_out, conv_b_out, attn_norm_g, w_qkv, b_qkv, q_norm_g,
              k_norm_g, sinks, w_o, b_o, rel_bias, mlp_norm_g, w_up, w_down):
    for i in range(DEPTH):
        j = i // N_MIXERS
        if i % N_MIXERS == 0:
            x = x + conformer_conv(x, conv_norm_g[j], conv_w_in[j], conv_b_in[j],
                                   conv_dw[j], conv_dw_b[j], conv_ln_g[j], conv_ln_b[j],
                                   conv_w_out[j], conv_b_out[j])
        else:
            x = x + swa_sink_attention(x, attn_norm_g[j], w_qkv[j], b_qkv[j],
                                       q_norm_g[j], k_norm_g[j], sinks[j], w_o[j],
                                       b_o[j], rel_bias)
        x = x + sq_relu_mlp(x, mlp_norm_g[i], w_up[i], w_down[i])
    return x


_drawn_inputs = setup_inputs


def setup_inputs(seed=0):
    import zlib

    import numpy as np

    out = dict(_drawn_inputs(seed))
    spreads = {}
    factors = {'conv_norm_g': 4.096,
     'conv_b_in': 4.003,
     'conv_ln_g': 3.842,
     'conv_ln_b': 4.53,
     'conv_b_out': 2.7,
     'attn_norm_g': 8.0,
     'b_qkv': 4.722,
     'q_norm_g': 8.0,
     'k_norm_g': 8.0,
     'sinks': 64.0,
     'b_o': 24.765}
    for name, (base, spread) in spreads.items():
        noise = np.random.default_rng([zlib.crc32(name.encode()), seed]).standard_normal(out[name].shape)
        drawn = base * np.exp(spread * noise) if base else spread * noise
        out[name] = __import__('jax').numpy.asarray(drawn.astype(out[name].dtype))
    for name, factor in factors.items():
        out[name] = (out[name] * factor).astype(out[name].dtype)
    return out
```

```python
from contextlib import ExitStack

import numpy as np

import concourse.bass as bass
from concourse import mybir

ALU = mybir.AluOpType
ACT = mybir.ActivationFunctionType
AX = mybir.AxisListType
F32 = mybir.dt.float32
F32R = mybir.dt.float32r

P = 128
D = 1024
T = 512
KT = D // P
TAPS = 31
PAD = TAPS - 1
HEADS = 16
HD = 64
BLOCKS = T // P
FF = 4 * D
HALF_TILES = FF // P // 2
EPS = 1e-6
NEG = -1e30
REL_BUCKETS = 32
REL_MAX_DIST = 128
CHUNK = 2 * P

C_IN = 0
C_OUT = C_IN + 2 * D // CHUNK
C_MLP0 = C_OUT + D // CHUNK
MLP_CHUNKS = FF // CHUNK + FF // D * D // CHUNK
C_KV = C_MLP0 + MLP_CHUNKS
C_Q = C_KV + 1
C_O = C_Q + D // CHUNK
C_MLP1 = C_O + D // CHUNK
CHUNKS = C_MLP1 + MLP_CHUNKS

_cols = dict(conv_g=KT, b_in=2 * KT, dw=TAPS * KT, dw_b=KT, ln_g=KT, ln_b=KT, b_out=KT, attn_g=KT,
             b_qkv=KT + 2, q_g=1, k_g=1, b_o=KT, mlp_g=2 * KT)
COL = {}
_at = 0
for _name, _n in _cols.items():
    COL[_name] = _at
    _at += _n
N_PAR = _at
N_CONST = P + P + P + 2
RV = 3 * P

BANK_CREDIT = 4
RELU_CREDIT = 2
GATE_CREDIT = 1
TAP_CREDIT = 1


def build(nc, w_all, x_t, params, consts, onehot, rel_bias, sinks, scratch, out):
    with ExitStack() as ctx:
        names = {}
        base = [(nc.sbuf_base + 63) // 64 * 64]

        def at(name, shape, dt, offset):
            assert offset + 4 * int(np.prod(shape[1:])) <= nc.sbuf_usable_end, name
            names[name] = (nc.alloc_sbuf_tensor_at(name, shape, dt, offset=offset), offset)
            return names[name][0]

        def sb(name, shape, dt=F32):
            offset = base[0]
            base[0] += (4 * int(np.prod(shape[1:])) + 31) // 32 * 32
            return at(name, shape, dt, offset)

        def sem(name):
            return ctx.enter_context(nc.semaphore(name))

        X = sb("residual", [P, KT, T])
        AH = sb("act_hi", [P, KT, T], F32R)
        AL = sb("act_lo", [P, KT, T], F32R)
        RAW = [sb(f"w_raw{s}", [P, KT, CHUNK]) for s in range(2)]
        WH = [sb(f"w_hi{s}", [P, KT, CHUNK], F32R) for s in range(2)]
        WL = [sb(f"w_lo{s}", [P, KT, CHUNK], F32R) for s in range(2)]
        PAR = sb("params", [P, N_PAR])
        CON = sb("consts", [P, N_CONST])
        ONES, IDENT, HEAD_ONES = CON[:, 0:P], CON[:, P:2 * P], CON[:, 2 * P:3 * P]
        HEAD_COLS = CON[:, 3 * P:3 * P + 2]
        SQ = sb("squares", [P, 2, T])
        SS = sb("square_sum", [P, T])
        Z = sb("mean_square", [P, T])
        R2 = sb("rstd_squared", [P, T])
        R = sb("rstd", [P, T])
        TM = sb("scaled", [P, 2, T])
        RB = sb("relu", [P, 2, T])
        VB = sb("relu_squared", [P, 2, T])
        BIAS = sb("bias", [P, HEADS, 2 * P])
        SINK = sb("sinks", [P, HEADS])
        GB = sb("q_gain_bias", [P, KT])
        region = base[0]
        HH = sb("hidden_hi", [P, HALF_TILES, T], F32R)
        HL = sb("hidden_lo", [P, HALF_TILES, T], F32R)
        region_end = base[0]

        base[0] = region
        U = sb("glu", [P, KT, PAD + T])
        Y = sb("conv", [P, KT, T])
        YS = sb("conv_sum", [P, T])
        VS = sb("conv_square_sum", [P, T])
        MU = sb("ln_mean", [P, T])
        RL = sb("ln_rstd", [P, T])
        TG = sb("gate_in", [P, T])
        SG = sb("gate", [P, T])
        TA = sb("glu_in", [P, T])
        ZL = sb("conv_act_lo", [P, KT, T], F32R)
        assert base[0] <= region_end
        ZH = at("conv_act_hi", [P, KT, T], F32R, region)
        base[0] = region
        OH = sb("attn_hi", [P, KT, T], F32R)
        OL = sb("attn_lo", [P, KT, T], F32R)
        KSH = sb("k_stack_hi", [P, 2, T], F32R)
        KSL = sb("k_stack_lo", [P, 2, T], F32R)
        VH = sb("v_hi", [P, BLOCKS, P], F32R)
        VL = sb("v_lo", [P, BLOCKS, P], F32R)
        QST = [sb(f"q_stack{s}", [P, 2, T], F32R) for s in range(2)]
        PH = [sb(f"probs_hi{s}", [P, 2, 2, P], F32R) for s in range(2)]
        PL = [sb(f"probs_lo{s}", [P, 2, 2, P], F32R) for s in range(2)]
        assert base[0] <= region_end
        base[0] = region_end
        LG = sb("logits", [P, 2, 2, 2 * P + 8])
        NM = sb("neg_max", [P, 2, 2])
        RS = sb("prob_sum", [P, 2, 2])
        RI = sb("prob_scale", [P, 2, 2])
        RQ = sb("q_scale", [P, 2, 2 * BLOCKS])
        QZ = sb("q_square_sum", [P, 4, 2 * BLOCKS])
        assert base[0] <= nc.sbuf_usable_end
        prep = names["relu_squared"][1]
        OHOT = at("onehot", [REL_BUCKETS, P], F32, prep)
        RELB = at("rel_bias_in", [REL_BUCKETS, HEADS], F32, prep + 4 * P)
        RVT = at("bias_rows", [HEADS, RV], F32, prep + 4 * (P + HEADS))

        PS = [ctx.enter_context(nc.psum_tensor(f"bank{b}", [P, T], F32)) for b in range(8)]

        x_landed = [sem(f"x_landed{q}") for q in range(4)]
        small_landed = sem("small_landed")
        w_landed = [sem(f"w_landed{s}") for s in range(2)]
        w_hi_done = sem("w_hi_done")
        w_split = sem("w_split")
        tile_mm = sem("tile_mm")
        a_hi = sem("a_hi")
        a_lo = sem("a_lo")
        sq_done = sem("sq_done")
        ss_acc = sem("ss_acc")
        stat_mm = sem("stat_mm")
        r2_done = sem("r2_done")
        r_done = sem("r_done")
        dve_step = sem("dve_step")
        pad_done = sem("pad_done")
        glu_free = sem("glu_free")
        gate_done, u_done, tap_done = sem("gate_done"), sem("u_done"), sem("tap_done")
        ys_acc, ln_mm, mu_done = sem("ys_acc"), sem("ln_mm"), sem("mu_done")
        yc_done, ysq_done, vs_acc = sem("yc_done"), sem("ysq_done"), sem("vs_acc")
        rl_inv, rl_done = sem("rl_inv"), sem("rl_done")
        yn_done, silu_done, z_hi, z_lo = sem("yn_done"), sem("silu_done"), sem("z_hi"), sem("z_lo")
        x_done = sem("x_done")
        tm_done = sem("tm_done")
        relu_done = sem("relu_done")
        hh_done, v_done, h_lo = sem("hh_done"), sem("v_done"), sem("h_lo")
        bias_mm, rows_done, rows_out, bias_in = (sem("bias_mm"), sem("rows_done"),
                                                 sem("rows_out"), sem("bias_in"))
        kv_scaled, k_biased, v_biased = (sem("kv_scaled"), sem("k_biased"),
                                                sem("v_biased"))
        k_sum_mm, k_inv, k_rstd, k_stacked = (sem("k_sum_mm"), sem("k_inv"), sem("k_rstd"),
                                              sem("k_stacked"))
        v_turned, vh_done, v_done_all = sem("v_turned"), sem("vh_done"), sem("v_split")
        q_scaled, q_biased, q_squared = (sem("q_scaled"), sem("q_biased"),
                                               sem("q_squared"))
        q_sum_mm, q_z, q_r0, q_r, q_stacked = (sem("q_sum_mm"), sem("q_z"), sem("q_r0"),
                                               sem("q_r"), sem("q_stacked"))
        s_mm, sink_in, l_done, e_done, p_done = (sem("s_mm"), sem("sink_in"), sem("l_done"),
                                                 sem("e_done"), sem("p_done"))
        t_mm, ph_done, pl_done, pv_mm = sem("t_mm"), sem("ph_done"), sem("pl_done"), sem("pv_mm")
        o_hi, o_lo = sem("o_hi"), sem("o_lo")
        out_done = sem("out_done")
        gb_done = sem("gb_done")
        act_step = sem("act_step")

        def par(name, i=0):
            return PAR[:, COL[name] + i:COL[name] + i + 1]

        def bias_of(head, lo):
            first = BIAS[:, head, 2 * P - 1 - lo:2 * P - lo]
            return bass.AP(first.tensor, first.offset, [first.ap[0], [-1, 2 * P - lo]])

        def parx(name, i):
            return PAR[:, bass.ds(COL[name] + i, 1)]

        R_IN, R_MLP0, R_ATT, R_MLP1 = range(4)
        SMALL = 5 * 16

        block = ctx.enter_context(nc.Block())

        @block.sync
        def _(sp):
            def load_x(q):
                sp.dma_start(X[:, 2 * q:2 * q + 2, :], x_t[:, 2 * q:2 * q + 2, :]).then_inc(x_landed[q], 16)

            load_x(0)
            load_x(1)
            sp.dma_start(RAW[0][:], w_all[0]).then_inc(w_landed[0], 16)
            load_x(2)
            load_x(3)
            sp.dma_start(RAW[1][:], w_all[1]).then_inc(w_landed[1], 16)
            with sp.Fori(1, CHUNKS // 2) as i:
                for s in range(2):
                    sp.wait_ge(w_split, 2 * i + s - 1)
                    sp.dma_start(RAW[s][:], w_all[bass.ds(2 * i + s, 1)].rearrange("a p k n -> (a p) k n")).then_inc(w_landed[s], 16)
            sp.wait_ge(w_split, CHUNKS - 2)
            sp.dma_start(RAW[0][:], w_all[CHUNKS - 1]).then_inc(w_landed[0], 16)
            for t in range(KT):
                sp.wait_ge(x_done, BANK_CREDIT + 5 * KT + t + 1)
                sp.dma_start(out[:, t, :], X[:, t, :]).then_inc(out_done, 16)
            sp.wait_ge(out_done, 16 * KT)

        def hi_of_chunk(act, c, s, landed, first=False):
            act.wait_ge(w_landed[s], 16 * landed)
            if not first:
                act.wait_ge(tile_mm, 2 * (c - 1))
            act.activation(WH[s][:], RAW[s][:], ACT.Copy).then_inc(w_hi_done, 1)

        def lo_of_chunk(eng, c, s, handover=False):
            if handover:
                eng.wait_ge(w_split, c)
            eng.wait_ge(w_hi_done, c + 1)
            eng.tensor_tensor(out=WL[s][:], in0=RAW[s][:], in1=WH[s][:].bitcast(F32),
                              op=ALU.subtract).then_inc(w_split, 1)

        def make_operand_act(act, rnd, k, j, gain):
            act.wait_ge(ss_acc, (KT + 1) * rnd + k)
            act.activation(AH[:, k, :], X[:, k, :], ACT.Identity, scale=gain).then_inc(a_hi, 1)
            act.activation(SQ[:, j, :], X[:, k, :], ACT.Square).then_inc(sq_done, 1)

        def make_operand_dve(dve, rnd, k, gain):
            dve.wait_ge(a_hi, KT * rnd + k + 1)
            dve.scalar_tensor_tensor(out=AL[:, k, :], in0=X[:, k, :], scalar=gain,
                                     in1=AH[:, k, :].bitcast(F32), op0=ALU.mult,
                                     op1=ALU.subtract).then_inc(a_lo, 1)

        def clear_sum(pool, rnd):
            if rnd:
                pool.wait_ge(stat_mm, rnd)
            pool.memset(SS[:], 0.0).then_inc(ss_acc, 1)

        def add_square(pool, rnd, k, j):
            pool.wait_ge(sq_done, KT * rnd + k + 1)
            pool.wait_ge(ss_acc, (KT + 1) * rnd + k + 1)
            pool.tensor_tensor(out=SS[:], in0=SS[:], in1=SQ[:, j, :], op=ALU.add).then_inc(ss_acc, 1)

        def product(pe, bank, s, j, k, bh, bl, start, stop):
            wh, wl = WH[s][:, k, j * P:(j + 1) * P], WL[s][:, k, j * P:(j + 1) * P]
            pe.matmul(bank, wh, bh, start=start, stop=False)
            pe.matmul(bank, wh, bl, start=False, stop=False)
            return pe.matmul(bank, wl, bh, start=False, stop=stop)

        def statistic(pe, rnd):
            pe.wait_ge(ss_acc, (KT + 1) * (rnd + 1))
            pe.matmul(PS[6][:], ONES, SS[:], start=True, stop=True).then_inc(stat_mm, 1)

        def rstd_squared(dve, rnd):
            dve.wait_ge(stat_mm, rnd + 1)
            step(dve, dve.tensor_scalar(Z[:], PS[6][:], 1.0 / D, EPS, ALU.mult, ALU.add))
            dve.reciprocal(R2[:], Z[:]).then_inc(r2_done, 1)

        steps = {}

        def step(eng, instr, s=dve_step):
            steps[s.name] = steps.get(s.name, 0) + 1
            instr.then_inc(s, 1)
            eng.wait_ge(s, steps[s.name])

        def project_pe(pe, c0, xb, bh, bl, ready, count):
            with pe.Fori(0, 2) as i:
                for s in range(2):
                    buf = (c0 + s) % 2
                    pe.wait_ge(w_split, c0 + 2 * i + s + 1)
                    for j in range(2):
                        pe.wait_ge(x_done, xb + 4 * i + 2 * s + j + 1)
                        for k in range(KT):
                            if s == 0 and j == 0:
                                pe.wait_ge(ready, count(k))
                            mm = product(pe, PS[2 * s + j][:], buf, j, k, bh[:, k, :], bl[:, k, :],
                                         k == 0, k == KT - 1)
                        mm.then_inc(tile_mm, 1)

        def project_act(act, c0, xb, rnd, gain):
            with act.Fori(0, 2) as i:
                for s in range(2):
                    hi_of_chunk(act, c0 + 2 * i + s + 1, (c0 + s + 1) % 2, (c0 + s + 1) // 2 + i + 1)
                    for j in range(2):
                        k = 4 * i + 2 * s + j
                        act.wait_ge(x_done, BANK_CREDIT + xb + k + 1)
                        make_operand_act(act, rnd, k, j, parx(*gain(k)))

        def project_dve(dve, c0, xb, rnd, bias, gain):
            with dve.Fori(0, 2) as i:
                for s in range(2):
                    for j in range(2):
                        k = 4 * i + 2 * s + j
                        dve.wait_ge(tile_mm, 2 * c0 + k + 1)
                        dve.scalar_tensor_tensor(out=X[:, k, :], in0=PS[2 * s + j][:], scalar=parx(bias, k),
                                                 in1=X[:, k, :], op0=ALU.add, op1=ALU.add).then_inc(x_done, 1)
                        make_operand_dve(dve, rnd, k, parx(*gain(k)))

        def project_pool(pool, c0, xb, rnd):
            clear_sum(pool, rnd)
            with pool.Fori(0, 2) as i:
                for s in range(2):
                    lo_of_chunk(pool, c0 + 2 * i + s + 1, (c0 + s + 1) % 2)
                    for j in range(2):
                        add_square(pool, rnd, 4 * i + 2 * s + j, j)

        def mlp_pe(pe, l, c0, xb, rnd):
            for half in range(2):
                h0 = (2 * l + half) * HALF_TILES
                c = c0 + half * MLP_CHUNKS // 2
                with pe.Fori(0, 4) as i:
                    for s in range(2):
                        pe.wait_ge(w_split, c + 2 * i + s + 1)
                        for j in range(2):
                            pe.wait_ge(relu_done, h0 + 4 * i + 2 * s + j + 1)
                            for k in range(KT):
                                if s == 0 and j == 0:
                                    pe.wait_ge(a_lo, KT * rnd + k + 1)
                                mm = product(pe, PS[2 * s + j][:], (c0 + s) % 2, j, k, AH[:, k, :],
                                             AL[:, k, :], k == 0, k == KT - 1)
                            mm.then_inc(tile_mm, 1)
                if half == 0:
                    statistic(pe, rnd)
                c += KT
                with pe.Fori(0, 4) as i:
                    for s in range(2):
                        pe.wait_ge(w_split, c + 2 * i + s + 1)
                        for j in range(2):
                            if s == 0:
                                pe.wait_ge(x_done, BANK_CREDIT + xb + half * KT + 2 * i + j - 1)
                            for k in range(KT):
                                if j == 0:
                                    pe.wait_ge(h_lo, h0 + KT * s + k + 1)
                                mm = product(pe, PS[4 + j][:], (c0 + s) % 2, j, k, HH[:, KT * s + k, :],
                                             HL[:, KT * s + k, :], s == 0 and k == 0, s == 1 and k == KT - 1)
                            mm.then_inc(tile_mm, 1)

        def mlp_act(act, l, c0, xb, nxt):
            for half in range(2):
                h0 = (2 * l + half) * HALF_TILES
                c = c0 + half * MLP_CHUNKS // 2
                with act.Fori(0, 4) as i:
                    for s in range(2):
                        hi_of_chunk(act, c + 2 * i + s + 1, (c0 + s + 1) % 2, (c + s + 1) // 2 + i + 1)
                        for j in range(2):
                            h = 4 * i + 2 * s + j
                            act.wait_ge(tile_mm, 2 * c + h + 1)
                            act.wait_ge(v_done, h0 + h + 1)
                            act.activation(RB[:, j, :], PS[2 * s + j][:], ACT.Relu).then_inc(relu_done, 1)
                            act.wait_ge(relu_done, BANK_CREDIT + h0 + h + 1)
                            act.activation(HH[:, h, :], RB[:, j, :], ACT.Square).then_inc(hh_done, 1)
                c += KT

                def down(i, last=False):
                    for s in range(2):
                        if not (last and s == 1):
                            hi_of_chunk(act, c + 2 * i + s + 1, (c0 + s + 1) % 2, (c + s + 1) // 2 + i + 1)
                    if half == 1 and nxt is not None:
                        for j in range(2):
                            act.wait_ge(x_done, BANK_CREDIT + xb + KT + 2 * i + j + 1)
                            make_operand_act(act, nxt[0], 2 * i + j, j, parx(nxt[1], 2 * i + j))

                if half == 1 and nxt is None:
                    with act.Fori(0, 3) as i:
                        down(i)
                    down(3, last=True)
                else:
                    with act.Fori(0, 4) as i:
                        down(i)

        def mlp_dve(dve, l, c0, xb, rnd, nxt):
            for half in range(2):
                h0 = (2 * l + half) * HALF_TILES
                c = c0 + half * MLP_CHUNKS // 2
                with dve.Fori(0, 4) as i:
                    for s in range(2):
                        lo_of_chunk(dve, c + 2 * i + s + 1, (c0 + s + 1) % 2, handover=True)
                        for j in range(2):
                            h = 4 * i + 2 * s + j
                            dve.wait_ge(relu_done, BANK_CREDIT + h0 + h + 1)
                            dve.tensor_tensor(out=VB[:, j, :], in0=RB[:, j, :], in1=RB[:, j, :],
                                              op=ALU.mult).then_inc(v_done, 1)
                            dve.wait_ge(v_done, RELU_CREDIT + h0 + h + 1)
                            dve.wait_ge(hh_done, h0 + h + 1)
                            dve.tensor_tensor(out=HL[:, h, :], in0=VB[:, j, :], in1=HH[:, h, :].bitcast(F32),
                                              op=ALU.subtract).then_inc(h_lo, 1)
                if half == 0:
                    rstd_squared(dve, rnd)
                    dve.wait_ge(r2_done, rnd + 1)
                c += KT

                def down(i, last=False):
                    for s in range(2):
                        if not (last and s == 1):
                            lo_of_chunk(dve, c + 2 * i + s + 1, (c0 + s + 1) % 2)
                    for j in range(2):
                        dve.wait_ge(tile_mm, 2 * (c + 2 * i + 1) + j + 1)
                        dve.tensor_tensor(out=TM[:, j, :], in0=PS[4 + j][:], in1=R2[:],
                                          op=ALU.mult).then_inc(tm_done, 1)
                        dve.wait_ge(tm_done, (2 * l + half) * KT + 2 * i + j + 1)
                        dve.tensor_tensor(out=X[:, 2 * i + j, :], in0=X[:, 2 * i + j, :], in1=TM[:, j, :],
                                          op=ALU.add).then_inc(x_done, 1)
                        if half == 1 and nxt is not None:
                            make_operand_dve(dve, nxt[0], 2 * i + j, parx(nxt[1], 2 * i + j))

                if half == 1 and nxt is None:
                    with dve.Fori(0, 3) as i:
                        down(i)
                    down(3, last=True)
                else:
                    with dve.Fori(0, 4) as i:
                        down(i)

        STEPS = KT * BLOCKS

        def keys_from(n):
            return P if n % BLOCKS == 0 else 0

        @block.tensor
        def _(pe):
            pe.wait_ge(small_landed, SMALL)
            pe.matmul(PS[7][0:HEADS, 0:P], RELB[:], OHOT[:], start=True, stop=True).then_inc(bias_mm, 1)

            def glu_chunk(m, s, first=False):
                pe.wait_ge(w_split, m + 1)
                for n, j in enumerate((1, 0)):
                    if not first:
                        pe.wait_ge(glu_free, 2 * m + n - 3)
                    for k in range(KT):
                        if first:
                            pe.wait_ge(a_lo, k + 1)
                        mm = product(pe, PS[2 * s + j][:], s, j, k, AH[:, k, :], AL[:, k, :],
                                     k == 0, k == KT - 1)
                    mm.then_inc(tile_mm, 1)

            glu_chunk(0, 0, first=True)
            statistic(pe, R_IN)
            glu_chunk(1, 1, first=True)
            with pe.Fori(1, KT // 2) as i:
                for s in range(2):
                    glu_chunk(2 * i + s, s)

            pe.wait_ge(ys_acc, KT + 1)
            pe.wait_ge(r2_done, 1)
            pe.matmul(PS[6][:], ONES, YS[:], start=True, stop=True).then_inc(ln_mm, 1)
            pe.wait_ge(vs_acc, KT + 1)
            pe.matmul(PS[7][:], ONES, VS[:], start=True, stop=True).then_inc(ln_mm, 1)

            project_pe(pe, C_OUT, 0, ZH, ZL, z_lo, lambda k: k + 1)
            mlp_pe(pe, 0, C_MLP0, KT, R_MLP0)

            pe.wait_ge(w_split, C_KV + 1)
            for j in range(2):
                for k in range(KT):
                    pe.wait_ge(a_lo, KT * R_ATT + k + 1)
                    mm = product(pe, PS[6 + j][:], C_KV % 2, j, k, AH[:, k, :], AL[:, k, :], k == 0, k == KT - 1)
                mm.then_inc(tile_mm, 1)
            pe.wait_ge(ss_acc, (KT + 1) * (R_ATT + 1))
            pe.matmul(PS[4][:], ONES, SS[:], start=True, stop=True).then_inc(stat_mm, 1)

            def q_part(jt, ks):
                c = C_Q + jt // 2
                if 0 in ks:
                    pe.wait_ge(w_split, c + 1)
                    if jt >= 2:
                        pe.wait_ge(q_z, jt - 1)
                for k in ks:
                    mm = product(pe, PS[jt % 2][:], c % 2, jt % 2, k, AH[:, k, :], AL[:, k, :],
                                 k == 0, k == KT - 1)
                if KT - 1 in ks:
                    mm.then_inc(tile_mm, 1)

            def q_sums(jt):
                pe.wait_ge(q_squared, jt + 1)
                for n in range(BLOCKS):
                    mm = pe.matmul(PS[jt % 2][:, 2 * n:2 * n + 2], RB[:, 1, n * P:(n + 1) * P], HEAD_COLS,
                                   start=True, stop=True)
                mm.then_inc(q_sum_mm, 1)

            q_part(0, range(KT))
            pe.wait_ge(k_biased, 2)
            pe.matmul(PS[5][:], HEAD_ONES, RB[:, 1, :], start=True, stop=True).then_inc(k_sum_mm, 1)
            pe.wait_ge(v_biased, 1)
            pe.wait_ge(r2_done, R_ATT + 1)
            for n in range(BLOCKS):
                mm = pe.transpose(PS[4][:, n * P:(n + 1) * P], VB[:, 0, n * P:(n + 1) * P], IDENT)
            mm.then_inc(v_turned, 1)
            q_part(1, range(KT))

            def scores(n):
                jt, b = n // BLOCKS, n % BLOCKS
                g, lo = jt // (KT // 2), keys_from(n)
                if b == 0:
                    pe.wait_ge(q_stacked, jt + 1)
                if n == 0:
                    pe.wait_ge(k_stacked, 1)
                if n >= 2:
                    pe.wait_ge(l_done, n - 1)
                first_key = (b - 1) * P + lo
                for e in range(2):
                    q = QST[jt % 2][:, e, b * P:(b + 1) * P]
                    o = PS[2 + n % 2][:, e * 2 * P + lo:(e + 1) * 2 * P]
                    pe.matmul(o, q, KSH[:, g, first_key:(b + 1) * P], start=True, stop=False)
                    mm = pe.matmul(o, q, KSL[:, g, first_key:(b + 1) * P], start=False, stop=True)
                mm.then_inc(s_mm, 1)

            def turn(n):
                pe.wait_ge(p_done, n + 1)
                if n >= 2:
                    pe.wait_ge(pl_done, n - 1)
                if n < 2:
                    pe.wait_ge(v_done_all, 1)
                for e in range(2):
                    for kb in range(keys_from(n) // P, 2):
                        mm = pe.transpose(PS[4 + n % 2][:, (2 * e + kb) * P:(2 * e + kb + 1) * P],
                                          LG[:, n % 2, e, kb * P:(kb + 1) * P], IDENT)
                mm.then_inc(t_mm, 1)

            def values(n):
                jt, b = n // BLOCKS, n % BLOCKS
                pe.wait_ge(pl_done, n + 1)
                if b % 2 == 0 and n >= 4:
                    pe.wait_ge(o_lo, n // 2 - 1)
                o = PS[6 + (n // 2) % 2][:, (b % 2) * 2 * P:(b % 2 + 1) * 2 * P]
                kbs = range(keys_from(n) // P, 2)
                for kb in kbs:
                    kblock = b - 1 + kb
                    ph, pl = PH[n % 2][:, :, kb, :], PL[n % 2][:, :, kb, :]
                    pe.matmul(o, VH[:, kblock, :], ph, start=kb == kbs[0], stop=False)
                    pe.matmul(o, VH[:, kblock, :], pl, start=False, stop=False)
                    mm = pe.matmul(o, VL[:, kblock, :], ph, start=False, stop=kb == 1)
                mm.then_inc(pv_mm, 1)

            q_sums(0)
            scores(0)
            for n in range(STEPS + 1):
                jt, b = n // BLOCKS, n % BLOCKS
                if jt + 2 < KT:
                    q_part(jt + 2, range(2 * b, 2 * b + 2))
                if b == 1 and jt + 1 < KT:
                    q_sums(jt + 1)
                if n + 1 < STEPS:
                    scores(n + 1)
                if n < STEPS:
                    turn(n)
                if n >= 1:
                    values(n - 1)

            project_pe(pe, C_O, 3 * KT, OH, OL, o_lo, lambda k: 2 * (k + 1))
            mlp_pe(pe, 1, C_MLP1, 4 * KT, R_MLP1)

        @block.scalar
        def _(act):
            for dst, src in ((PAR, params), (CON, consts), (OHOT, onehot), (RELB, rel_bias)):
                act.dma_start(dst[:], src).then_inc(small_landed, 16)
            act.dma_start(SINK[:], sinks.broadcast_to([P, HEADS])).then_inc(small_landed, 16)
            act.wait_ge(small_landed, SMALL)
            for k in range(KT):
                act.wait_ge(x_landed[k // 2], 16)
                make_operand_act(act, R_IN, k, k % 2, par("conv_g", k))
                if k == 1:
                    hi_of_chunk(act, 0, 0, 1, first=True)

            def glu(m, s, landed):
                hi_of_chunk(act, m + 1, 1 - s, landed)
                act.wait_ge(glu_free, 2 * m + 1)
                act.wait_ge(u_done, m)
                act.activation(SG[:], TG[:], ACT.Sigmoid, bias=parx("b_in", KT + m)).then_inc(gate_done, 1)

            hi_of_chunk(act, 1, 1, 1, first=True)
            act.wait_ge(r2_done, 1)
            act.activation(R[:], R2[:], ACT.Sqrt).then_inc(r_done, 1)
            act.wait_ge(glu_free, 1)
            act.activation(SG[:], TG[:], ACT.Sigmoid, bias=par("b_in", KT)).then_inc(gate_done, 1)
            glu(1, 1, 2)
            with act.Fori(1, KT // 2) as i:
                for s in range(2):
                    glu(2 * i + s, s, i + 1 + s)

            act.wait_ge(ln_mm, 1)
            act.activation(MU[:], PS[6][:], ACT.Copy, scale=1.0 / D).then_inc(mu_done, 1)
            act.wait_ge(ss_acc, KT + 1)
            for m in range(KT):
                act.wait_ge(yc_done, m + 1)
                if m >= 2:
                    act.wait_ge(vs_acc, m)
                act.activation(SQ[:, m % 2, :], Y[:, m, :], ACT.Square).then_inc(ysq_done, 1)
            act.wait_ge(rl_inv, 1)
            act.activation(RL[:], MU[:], ACT.Sqrt).then_inc(rl_done, 1)
            for m in range(KT):
                act.wait_ge(yn_done, m + 1)
                act.activation(Y[:, m, :], Y[:, m, :], ACT.Silu, bias=par("ln_b", m),
                               scale=par("ln_g", m)).then_inc(silu_done, 1)
                act.wait_ge(silu_done, m + 1)
                act.activation(ZH[:, m, :], Y[:, m, :], ACT.Copy).then_inc(z_hi, 1)

            project_act(act, C_OUT, 0, R_MLP0, lambda k: ("mlp_g", k))
            mlp_act(act, 0, C_MLP0, KT, (R_ATT, "attn_g"))

            for jt in range(KT):
                ins = act.activation(GB[:, jt:jt + 1], par("b_qkv", 2 + jt), ACT.Identity, scale=par("q_g"))
            ins.then_inc(gb_done, 1)
            hi_of_chunk(act, C_Q, C_Q % 2, C_Q // 2 + 1)
            act.wait_ge(r2_done, R_ATT + 1)
            act.activation(R[:], R2[:], ACT.Sqrt).then_inc(r_done, 1)
            act.wait_ge(kv_scaled, 1)
            act.activation(RB[:, 0, :], TM[:, 0, :], ACT.Identity, bias=par("b_qkv", 0)).then_inc(k_biased, 1)
            act.activation(RB[:, 1, :], TM[:, 0, :], ACT.Square, bias=par("b_qkv", 0)).then_inc(k_biased, 1)
            act.wait_ge(kv_scaled, 2)
            act.activation(VB[:, 0, :], TM[:, 1, :], ACT.Identity, bias=par("b_qkv", 1)).then_inc(v_biased, 1)
            act.wait_ge(k_inv, 1)
            act.activation(Z[:], VB[:, 1, :], ACT.Sqrt).then_inc(k_rstd, 1)
            act.wait_ge(v_turned, 1)
            act.activation(VH[:], PS[4][:].rearrange("p (n d) -> p n d", n=BLOCKS), ACT.Copy).then_inc(vh_done, 1)
            act.wait_ge(gb_done, 1)

            def q_bias(jt):
                act.wait_ge(q_scaled, jt + 1)
                if jt:
                    act.wait_ge(q_stacked, jt)
                else:
                    act.wait_ge(k_stacked, 1)
                act.activation(RB[:, 0, :], TM[:, 0, :], ACT.Identity, bias=GB[:, jt:jt + 1],
                               scale=par("q_g")).then_inc(q_biased, 1)
                if jt:
                    act.wait_ge(q_sum_mm, jt)
                else:
                    act.wait_ge(k_sum_mm, 1)
                act.activation(RB[:, 1, :], TM[:, 0, :], ACT.Square, bias=par("b_qkv", 2 + jt)).then_inc(q_squared, 1)

            def q_rsqrt(jt):
                act.wait_ge(q_z, jt + 1)
                if jt:
                    act.wait_ge(q_r, jt)
                act.activation(QZ[:, 1, :], QZ[:, 0, :], ACT.Ln).then_inc(act_step, 1)
                act.wait_ge(act_step, jt + 1)
                act.activation(QZ[:, 2, :], QZ[:, 1, :], ACT.Exp, scale=-0.5).then_inc(q_r0, 1)

            def exps(n):
                act.wait_ge(l_done, n + 1)
                lo = keys_from(n)
                if n >= 2:
                    act.wait_ge(p_done, n - 1)
                for e in range(2):
                    row = LG[:, n % 2, e, lo:2 * P + 1]
                    ins = act.activation(row, row, ACT.Exp, bias=NM[:, n % 2, e:e + 1],
                                         accum_out=RS[:, n % 2, e:e + 1])
                ins.then_inc(e_done, 1)

            def probs_hi(n):
                act.wait_ge(t_mm, n + 1)
                if n >= 2:
                    act.wait_ge(pv_mm, n - 1)
                kb = keys_from(n) // P
                t = PS[4 + n % 2][:].rearrange("p (e k q) -> p e k q", e=2, k=2)
                act.activation(PH[n % 2][:, :, kb:2, :], t[:, :, kb:2, :], ACT.Copy).then_inc(ph_done, 1)

            def outs_hi(p):
                act.wait_ge(pv_mm, 2 * p + 2)
                jt, half = p // 2, p % 2
                g = jt // (KT // 2)
                o = PS[6 + p % 2][g * HD:(g + 1) * HD, :].rearrange("p (n e q) -> p n e q", n=2, e=2)
                for e in range(2):
                    dst = OH[e * HD:(e + 1) * HD, jt, half * 2 * P:(half + 1) * 2 * P]
                    ins = act.activation(dst.rearrange("p (n q) -> p n q", n=2), o[:, :, e, :], ACT.Copy)
                ins.then_inc(o_hi, 1)

            q_bias(0)
            q_rsqrt(0)
            exps(0)
            for n in range(STEPS + 1):
                jt, b = n // BLOCKS, n % BLOCKS
                if b == 0 and jt + 1 < KT:
                    q_bias(jt + 1)
                if b == 2 and jt + 1 < KT:
                    q_rsqrt(jt + 1)
                if b == 0 and jt % 2 == 0 and C_Q + jt // 2 + 1 < C_O + 1 and jt < KT:
                    c = C_Q + jt // 2 + 1
                    hi_of_chunk(act, c, c % 2, c // 2 + 1)
                if n + 1 < STEPS:
                    exps(n + 1)
                if n < STEPS:
                    probs_hi(n)
                if n >= 2 and n % 2 == 0:
                    outs_hi(n // 2 - 1)

            project_act(act, C_O, 3 * KT, R_MLP1, lambda k: ("mlp_g", KT + k))
            mlp_act(act, 1, C_MLP1, 4 * KT, None)

        @block.vector
        def _(dve):
            dve.sem_inc(x_done, BANK_CREDIT)
            dve.sem_inc(relu_done, BANK_CREDIT)
            dve.sem_inc(v_done, RELU_CREDIT)
            dve.sem_inc(gate_done, GATE_CREDIT)
            dve.sem_inc(tap_done, TAP_CREDIT)
            dve.memset(U[:, :, 0:PAD], 0.0).then_inc(pad_done, 1)
            dve.wait_ge(pad_done, 1)
            dve.wait_ge(small_landed, SMALL)
            for k in range(KT):
                make_operand_dve(dve, R_IN, k, par("conv_g", k))
                if k == 1:
                    lo_of_chunk(dve, 0, 0)
            step(dve, dve.memset(RVT[:], NEG))
            dve.wait_ge(bias_mm, 1)
            dve.tensor_copy(RVT[:, P - 1:2 * P - 1], PS[7][0:HEADS, 0:P]).then_inc(rows_done, 1)
            rstd_squared(dve, R_IN)
            dve.wait_ge(r_done, 1)

            def glu_and_conv(m, s):
                dve.wait_ge(tile_mm, 2 * m + 1)
                dve.wait_ge(gate_done, GATE_CREDIT + m)
                dve.tensor_tensor(out=TG[:], in0=PS[2 * s + 1][:], in1=R[:], op=ALU.mult).then_inc(glu_free, 1)
                dve.wait_ge(tile_mm, 2 * m + 2)
                dve.tensor_tensor(out=TA[:], in0=PS[2 * s][:], in1=R[:], op=ALU.mult).then_inc(glu_free, 1)
                dve.wait_ge(glu_free, 2 * m + 2)
                dve.wait_ge(gate_done, GATE_CREDIT + m + 1)
                dve.scalar_tensor_tensor(out=U[:, m, PAD:PAD + T], in0=TA[:], scalar=parx("b_in", m), in1=SG[:],
                                         op0=ALU.add, op1=ALU.mult).then_inc(u_done, 1)
                dve.wait_ge(u_done, m + 1)
                n = 0
                for tap in range(TAPS):
                    src, w, acc = U[:, m, tap:tap + T], parx("dw", tap * KT + m), PS[4 + tap % 2][:]
                    dve.wait_ge(tap_done, TAP_CREDIT + (TAPS + 1) * m + max(n - 1, 0))
                    if tap == 0:
                        ins = dve.tensor_scalar(acc, src, w, parx("dw_b", m), ALU.mult, ALU.add)
                    elif tap == 1:
                        ins = dve.tensor_scalar(acc, src, w, None, ALU.mult)
                    else:
                        dst = Y[:, m, :] if tap == TAPS - 1 else acc
                        ins = dve.scalar_tensor_tensor(out=dst, in0=src, scalar=w, in1=acc, op0=ALU.mult, op1=ALU.add)
                    ins.then_inc(tap_done, 1)
                    n += 1
                dve.wait_ge(tap_done, TAP_CREDIT + (TAPS + 1) * m + TAPS)
                dve.tensor_tensor(out=Y[:, m, :], in0=Y[:, m, :], in1=PS[5][:], op=ALU.add).then_inc(tap_done, 1)

            with dve.Fori(0, KT // 2) as i:
                for s in range(2):
                    glu_and_conv(2 * i + s, s)

            dve.wait_ge(mu_done, 1)
            dve.wait_ge(tap_done, TAP_CREDIT + (TAPS + 1) * KT)
            for m in range(KT):
                dve.tensor_tensor(out=Y[:, m, :], in0=Y[:, m, :], in1=MU[:], op=ALU.subtract).then_inc(yc_done, 1)
            dve.wait_ge(ln_mm, 2)
            step(dve, dve.tensor_scalar(Z[:], PS[7][:], 1.0 / D, EPS, ALU.mult, ALU.add))
            dve.wait_ge(yc_done, KT)
            dve.reciprocal(MU[:], Z[:]).then_inc(rl_inv, 1)
            dve.wait_ge(rl_done, 1)
            for m in range(KT):
                dve.wait_ge(ysq_done, m + 1)
                dve.tensor_tensor(out=Y[:, m, :], in0=Y[:, m, :], in1=RL[:], op=ALU.mult).then_inc(yn_done, 1)
            for m in range(KT):
                dve.wait_ge(z_hi, m + 1)
                dve.tensor_tensor(out=ZL[:, m, :], in0=Y[:, m, :], in1=ZH[:, m, :].bitcast(F32),
                                  op=ALU.subtract).then_inc(z_lo, 1)

            project_dve(dve, C_OUT, 0, R_MLP0, "b_out", lambda k: ("mlp_g", k))
            mlp_dve(dve, 0, C_MLP0, KT, R_MLP0, (R_ATT, "attn_g"))

            dve.wait_ge(stat_mm, R_ATT + 1)
            step(dve, dve.tensor_scalar(Z[:], PS[4][:], 1.0 / D, EPS, ALU.mult, ALU.add))
            dve.reciprocal(R2[:], Z[:]).then_inc(r2_done, 1)
            dve.wait_ge(r_done, 2)
            for j in range(2):
                dve.wait_ge(tile_mm, 2 * C_KV + j + 1)
                dve.tensor_tensor(out=TM[:, j, :], in0=PS[6 + j][:], in1=R[:], op=ALU.mult).then_inc(kv_scaled, 1)
            dve.wait_ge(k_sum_mm, 1)
            step(dve, dve.tensor_scalar(Z[:], PS[5][:], 1.0 / HD, EPS, ALU.mult, ALU.add))
            dve.reciprocal(VB[:, 1, :], Z[:]).then_inc(k_inv, 1)
            dve.wait_ge(k_rstd, 1)
            dve.wait_ge(k_biased, 1)
            step(dve, dve.scalar_tensor_tensor(out=VB[:, 1, :], in0=RB[:, 0, :], scalar=par("k_g"), in1=Z[:],
                                               op0=ALU.mult, op1=ALU.mult))
            for g in range(2):
                src = VB[g * HD:(g + 1) * HD, 1, :]
                for h in range(2):
                    ins = dve.tensor_copy(KSH[h * HD:(h + 1) * HD, g, :], src)
            step(dve, ins)
            for g in range(2):
                src = VB[g * HD:(g + 1) * HD, 1, :]
                for h in range(2):
                    ins = dve.tensor_tensor(out=KSL[h * HD:(h + 1) * HD, g, :], in0=src,
                                            in1=KSH[g * HD:(g + 1) * HD, g, :].bitcast(F32), op=ALU.subtract)
            ins.then_inc(k_stacked, 1)
            dve.wait_ge(vh_done, 1)
            dve.tensor_tensor(out=VL[:], in0=PS[4][:].rearrange("p (n d) -> p n d", n=BLOCKS),
                              in1=VH[:].bitcast(F32), op=ALU.subtract).then_inc(v_done_all, 1)

            def q_scale(jt):
                dve.wait_ge(tile_mm, 2 * C_Q + jt + 1)
                if jt:
                    dve.wait_ge(q_squared, jt)
                else:
                    dve.wait_ge(k_biased, 2)
                dve.tensor_tensor(out=TM[:, 0, :], in0=PS[jt % 2][:], in1=R[:], op=ALU.mult).then_inc(q_scaled, 1)

            def q_norm(jt):
                dve.wait_ge(q_sum_mm, jt + 1)
                if jt:
                    dve.wait_ge(q_r, jt)
                dve.tensor_scalar(QZ[:, 0, :], PS[jt % 2][:, 0:2 * BLOCKS], float(HD * EPS), None,
                                  ALU.add).then_inc(q_z, 1)
                dve.wait_ge(q_biased, jt + 1)
                if jt >= 2:
                    dve.wait_ge(s_mm, BLOCKS * (jt - 1))
                st = QST[jt % 2]
                dve.tensor_copy(st[0:HD, 0, :], RB[0:HD, 0, :])
                step(dve, dve.tensor_copy(st[HD:P, 1, :], RB[HD:P, 0, :]))
                dve.tensor_tensor(out=st[HD:P, 0, :], in0=RB[0:HD, 0, :], in1=st[0:HD, 0, :].bitcast(F32),
                                  op=ALU.subtract)
                dve.tensor_tensor(out=st[0:HD, 1, :], in0=RB[HD:P, 0, :], in1=st[HD:P, 1, :].bitcast(F32),
                                  op=ALU.subtract).then_inc(q_stacked, 1)
                dve.wait_ge(q_r0, jt + 1)
                step(dve, dve.tensor_tensor(out=QZ[:, 3, :], in0=QZ[:, 0, :], in1=QZ[:, 2, :], op=ALU.mult))
                step(dve, dve.scalar_tensor_tensor(out=QZ[:, 3, :], in0=QZ[:, 3, :], scalar=-0.5, in1=QZ[:, 2, :],
                                                   op0=ALU.mult, op1=ALU.mult))
                dve.scalar_tensor_tensor(out=RQ[:, jt % 2, :], in0=QZ[:, 3, :], scalar=1.5, in1=QZ[:, 2, :],
                                         op0=ALU.add, op1=ALU.mult).then_inc(q_r, 1)

            def logits(n):
                jt, b, lo = n // BLOCKS, n % BLOCKS, keys_from(n)
                dve.wait_ge(s_mm, n + 1)
                dve.wait_ge(sink_in, n + 1)
                if b == 0:
                    dve.wait_ge(q_r, jt + 1)
                for e in range(2):
                    ins = dve.scalar_tensor_tensor(
                        out=LG[:, n % 2, e, lo:2 * P], in0=PS[2 + n % 2][:, e * 2 * P + lo:(e + 1) * 2 * P],
                        scalar=RQ[:, jt % 2, 2 * b + e:2 * b + e + 1], in1=bias_of(2 * jt + e, lo),
                        op0=ALU.mult, op1=ALU.add)
                step(dve, ins)
                dve.tensor_reduce(NM[:, n % 2, :], LG[:, n % 2, :, lo:2 * P + 1], AX.X, ALU.max,
                                  negate=True).then_inc(l_done, 1)

            def normalise(n):
                lo = keys_from(n)
                dve.wait_ge(e_done, n + 1)
                step(dve, dve.reciprocal(RI[:, n % 2, :], RS[:, n % 2, :]))
                for e in range(2):
                    row = LG[:, n % 2, e, lo:2 * P]
                    ins = dve.tensor_scalar(row, row, RI[:, n % 2, e:e + 1], None, ALU.mult)
                ins.then_inc(p_done, 1)

            def probs_lo(n):
                dve.wait_ge(ph_done, n + 1)
                kb = keys_from(n) // P
                t = PS[4 + n % 2][:].rearrange("p (e k q) -> p e k q", e=2, k=2)
                dve.tensor_tensor(out=PL[n % 2][:, :, kb:2, :], in0=t[:, :, kb:2, :],
                                  in1=PH[n % 2][:, :, kb:2, :].bitcast(F32), op=ALU.subtract).then_inc(pl_done, 1)

            def outs_lo(p):
                dve.wait_ge(o_hi, p + 1)
                jt, half = p // 2, p % 2
                g = jt // (KT // 2)
                o = PS[6 + p % 2][g * HD:(g + 1) * HD, :].rearrange("p (n e q) -> p n e q", n=2, e=2)
                for e in range(2):
                    at_ = (slice(e * HD, (e + 1) * HD), jt, slice(half * 2 * P, (half + 1) * 2 * P))
                    ins = dve.tensor_tensor(out=OL[at_].rearrange("p (n q) -> p n q", n=2), in0=o[:, :, e, :],
                                            in1=OH[at_].rearrange("p (n q) -> p n q", n=2).bitcast(F32),
                                            op=ALU.subtract)
                ins.then_inc(o_lo, 1)

            q_scale(0)
            q_norm(0)
            dve.wait_ge(bias_in, 16)
            logits(0)
            for n in range(STEPS + 1):
                jt, b = n // BLOCKS, n % BLOCKS
                if b == 0 and jt + 1 < KT:
                    q_scale(jt + 1)
                if b == 2 and jt + 1 < KT:
                    q_norm(jt + 1)
                if n + 1 < STEPS:
                    logits(n + 1)
                if n < STEPS:
                    normalise(n)
                if n >= 1:
                    probs_lo(n - 1)
                if n >= 3 and n % 2 == 1:
                    outs_lo((n - 3) // 2)
            outs_lo(STEPS // 2 - 1)

            project_dve(dve, C_O, 3 * KT, R_MLP1, "b_o", lambda k: ("mlp_g", KT + k))
            mlp_dve(dve, 1, C_MLP1, 4 * KT, R_MLP1, None)

        @block.gpsimd
        def _(pool):
            clear_sum(pool, R_IN)
            for k in range(KT):
                add_square(pool, R_IN, k, k % 2)
            pool.memset(YS[:], 0.0).then_inc(ys_acc, 1)
            pool.memset(VS[:], 0.0).then_inc(vs_acc, 1)
            pool.wait_ge(rows_done, 1)
            pool.dma_start(scratch, RVT[:]).then_inc(rows_out, 16)
            pool.wait_ge(rows_out, 16)
            pool.dma_start(BIAS[:], bass.AP(scratch.tensor, 0, [[1, P], [RV, HEADS], [1, 2 * P]])
                           ).then_inc(bias_in, 16)
            lo_of_chunk(pool, 1, 1, handover=True)

            def add_conv(m, s):
                lo_of_chunk(pool, m + 2, s)
                pool.wait_ge(tap_done, TAP_CREDIT + (TAPS + 1) * (m + 1))
                pool.wait_ge(ys_acc, m + 1)
                pool.tensor_tensor(out=YS[:], in0=YS[:], in1=Y[:, m, :], op=ALU.add).then_inc(ys_acc, 1)

            with pool.Fori(0, KT // 2 - 1) as i:
                for s in range(2):
                    add_conv(2 * i + s, s)
            add_conv(KT - 2, 0)
            pool.wait_ge(tap_done, TAP_CREDIT + (TAPS + 1) * KT)
            pool.wait_ge(ys_acc, KT)
            pool.tensor_tensor(out=YS[:], in0=YS[:], in1=Y[:, KT - 1, :], op=ALU.add).then_inc(ys_acc, 1)
            for m in range(KT):
                pool.wait_ge(ysq_done, m + 1)
                pool.wait_ge(vs_acc, m + 1)
                pool.tensor_tensor(out=VS[:], in0=VS[:], in1=SQ[:, m % 2, :], op=ALU.add).then_inc(vs_acc, 1)

            project_pool(pool, C_OUT, 0, R_MLP0)
            clear_sum(pool, R_ATT)
            with pool.Fori(0, KT // 2) as i:
                for j in range(2):
                    add_square(pool, R_ATT, 2 * i + j, j)
            lo_of_chunk(pool, C_Q, C_Q % 2, handover=True)

            def sink(n):
                jt = n // BLOCKS
                if n >= 2:
                    pool.wait_ge(t_mm, n - 1)
                pool.tensor_copy(LG[:, n % 2, :, 2 * P:2 * P + 1],
                                 SINK[:, 2 * jt:2 * jt + 2].rearrange("p (e a) -> p e a", a=1)).then_inc(sink_in, 1)

            sink(0)
            for n in range(STEPS):
                if n % (2 * BLOCKS) == 0:
                    c = C_Q + n // (2 * BLOCKS) + 1
                    lo_of_chunk(pool, c, c % 2)
                if n + 1 < STEPS:
                    sink(n + 1)
            project_pool(pool, C_O, 3 * KT, R_MLP1)


def kernel(**inputs):
    import math
    import concourse.bacc as bacc
    from concourse.bass_utils import run_bass_kernel_spmd

    a = {name: np.asarray(value) for name, value in inputs.items()}

    def chunked(w, *starts):
        cols = [w[:, c:c + P].reshape(KT, P, P).transpose(1, 0, 2) for c in starts]
        return np.concatenate(cols, axis=2)

    def projection(w, first=0):
        return [chunked(w, c, c + P) for c in range(first, first + D, CHUNK)]

    def mlp(up, down):
        chunks = []
        for half in range(2):
            h = half * FF // 2
            chunks += [chunked(up, c, c + P) for c in range(h, h + FF // 2, CHUNK)]
            chunks += [chunked(down[r:r + D], c, c + P) for c in range(0, D, CHUNK)
                       for r in range(h, h + FF // 2, D)]
        return chunks

    w_in, w_qkv = a["conv_w_in"][0], a["w_qkv"][0]
    chunks = [chunked(w_in, c, D + c) for c in range(0, D, P)]
    chunks += projection(a["conv_w_out"][0])
    chunks += mlp(a["w_up"][0], a["w_down"][0])
    chunks += [chunked(w_qkv, D, D + P)] + projection(w_qkv) + projection(a["w_o"][0])
    chunks += mlp(a["w_up"][1], a["w_down"][1])
    assert len(chunks) == CHUNKS

    def rows(v):
        return v.reshape(-1, P)

    b_qkv = rows(a["b_qkv"][0])
    parts = [rows(a["conv_norm_g"][0]), rows(a["conv_b_in"][0]), rows(a["conv_dw"][0]), rows(a["conv_dw_b"][0]),
             rows(a["conv_ln_g"][0]), rows(a["conv_ln_b"][0]), rows(a["conv_b_out"][0]), rows(a["attn_norm_g"][0]),
             b_qkv[KT:], b_qkv[:KT], rows(np.tile(a["q_norm_g"][0], 2)), rows(np.tile(a["k_norm_g"][0], 2)),
             rows(a["b_o"][0]), rows(a["mlp_norm_g"])]

    head = np.arange(P) // HD
    consts = np.concatenate([np.ones((P, P)), np.eye(P), head[:, None] == head[None, :],
                             head[:, None] == np.arange(2)[None, :]], axis=1).astype(np.float32)
    dist = np.arange(P)
    exact = REL_BUCKETS // 2
    large = exact + (np.log(np.maximum(dist, 1).astype(np.float32) / exact) / math.log(REL_MAX_DIST / exact)
                     * (REL_BUCKETS - exact)).astype(np.int32)
    bucket = np.where(dist < exact, dist, np.minimum(large, REL_BUCKETS - 1))
    onehot = (np.arange(REL_BUCKETS)[:, None] == bucket[None, :]).astype(np.float32)

    arrays = {
        "w_all": np.stack(chunks),
        "x_t": np.ascontiguousarray(a["x"][0].T.reshape(KT, P, T).transpose(1, 0, 2)),
        "params": np.ascontiguousarray(np.concatenate(parts).T),
        "consts": consts,
        "onehot": onehot,
        "rel_bias": np.ascontiguousarray(a["rel_bias"]),
        "sinks": np.ascontiguousarray(a["sinks"]),
    }
    nc = bacc.Bacc("TRN2", target_bir_lowering=False, num_devices=1)
    args = [nc.dram_tensor(f"in_{n}", v.shape, mybir.dt.from_np(v.dtype), kind="ExternalInput").ap()
            for n, v in arrays.items()]
    scratch = nc.dram_tensor("bias_scratch", (HEADS, RV), F32, kind="Internal").ap()
    out = nc.dram_tensor("out_t", (P, KT, T), F32, kind="ExternalOutput").ap()
    build(nc, *args, scratch, out)
    got = run_bass_kernel_spmd(nc, [{f"in_{n}": v for n, v in arrays.items()}], core_ids=[0]).results[0]["out_t"]
    return got.transpose(1, 0, 2).reshape(D, T).T.reshape(1, T, D)
```

```python
from contextlib import ExitStack

import numpy as np

import concourse.bass as bass
from concourse import mybir

ALU = mybir.AluOpType
ACT = mybir.ActivationFunctionType
AX = mybir.AxisListType
F32 = mybir.dt.float32
F32R = mybir.dt.float32r

P = 128
D = 1024
T = 512
KT = D // P
TAPS = 31
PAD = TAPS - 1
HEADS = 16
HD = 64
BLOCKS = T // P
FF = 4 * D
HALF_TILES = FF // P // 2
EPS = 1e-6
NEG = -1e30
REL_BUCKETS = 32
REL_MAX_DIST = 128
CHUNK = 2 * P

C_IN = 0
C_OUT = C_IN + 2 * D // CHUNK
C_MLP0 = C_OUT + D // CHUNK
MLP_CHUNKS = FF // CHUNK + FF // D * D // CHUNK
C_KV = C_MLP0 + MLP_CHUNKS
C_Q = C_KV + 1
C_O = C_Q + D // CHUNK
C_MLP1 = C_O + D // CHUNK
CHUNKS = C_MLP1 + MLP_CHUNKS

_cols = dict(conv_g=KT, b_in=2 * KT, dw=TAPS * KT, dw_b=KT, ln_g=KT, ln_b=KT, b_out=KT, attn_g=KT,
             b_qkv=KT + 2, q_g=1, k_g=1, b_o=KT, mlp_g=2 * KT)
COL = {}
_at = 0
for _name, _n in _cols.items():
    COL[_name] = _at
    _at += _n
N_PAR = _at
N_CONST = P + P + P + 2
RV = 3 * P

BANK_CREDIT = 4
RELU_CREDIT = 2
GATE_CREDIT = 1
PE_CONV_CREDIT = 1
PRODUCT_CREDIT = 2

POOL_TAPS = 7
PE_TAPS = 7
DVE_TAPS = TAPS - POOL_TAPS - PE_TAPS
PE_FIRST = POOL_TAPS
DVE_FIRST = POOL_TAPS + PE_TAPS
DVE_STEPS = DVE_TAPS + 1
POOL_SUM_AT = 7
GATE_AFTER, VALUE_AFTER, LO_AFTER = 1, 4, 9
TAP_CREDIT = 2 * DVE_STEPS

RING = 3


def build(nc, w_all, x_t, params, consts, onehot, rel_bias, sinks, scratch, out):
    with ExitStack() as ctx:
        names = {}
        base = [(nc.sbuf_base + 63) // 64 * 64]

        def at(name, shape, dt, offset):
            assert offset + 4 * int(np.prod(shape[1:])) <= nc.sbuf_usable_end, name
            names[name] = (nc.alloc_sbuf_tensor_at(name, shape, dt, offset=offset), offset)
            return names[name][0]

        def sb(name, shape, dt=F32):
            offset = base[0]
            base[0] += (4 * int(np.prod(shape[1:])) + 31) // 32 * 32
            return at(name, shape, dt, offset)

        def sem(name):
            return ctx.enter_context(nc.semaphore(name))

        X = sb("residual", [P, KT, T])
        AH = sb("act_hi", [P, KT, T], F32R)
        AL = sb("act_lo", [P, KT, T], F32R)
        RAW = [sb(f"w_raw{s}", [P, KT, CHUNK]) for s in range(2)]
        WH = [sb(f"w_hi{s}", [P, KT, CHUNK], F32R) for s in range(2)]
        WL = [sb(f"w_lo{s}", [P, KT, CHUNK], F32R) for s in range(2)]
        PAR = sb("params", [P, N_PAR])
        CON = sb("consts", [P, N_CONST])
        ONES, IDENT, HEAD_ONES = CON[:, 0:P], CON[:, P:2 * P], CON[:, 2 * P:3 * P]
        HEAD_COLS = CON[:, 3 * P:3 * P + 2]
        SQ = sb("squares", [P, 2, T])
        SS = sb("square_sum", [P, T])
        Z = sb("mean_square", [P, T])
        R2 = sb("rstd_squared", [P, T])
        R = sb("rstd", [P, T])
        TM = sb("scaled", [P, 2, T])
        RB = sb("relu", [P, 2, T])
        VB = sb("relu_squared", [P, 2, T])
        BIAS = sb("bias", [P, HEADS, 2 * P])
        SINK = sb("sinks", [P, HEADS])
        GB = sb("q_gain_bias", [P, KT])
        region = base[0]
        HH = sb("hidden_hi", [P, HALF_TILES, T], F32R)
        HL = sb("hidden_lo", [P, HALF_TILES, T], F32R)
        region_end = base[0]

        base[0] = region
        Y = sb("conv", [P, KT, T])
        YS = sb("conv_sum", [P, T])
        MU = sb("ln_mean", [P, T])
        RL = sb("ln_rstd", [P, T])
        TG = sb("gate_in", [P, T])
        SG = sb("gate", [P, T])
        TA = sb("glu_in", [P, T])
        ZH = sb("conv_act_hi", [P, KT, T], F32R)
        ZL = sb("conv_act_lo", [P, KT, T], F32R)
        assert base[0] <= region_end
        GLU_LEN = PAD + T
        assert base[0] <= region_end
        base[0] = names["conv_act_hi"][1]
        U = [sb(f"glu{s}", [P, GLU_LEN]) for s in range(2)]
        DWH = sb("dw_hi", [P, PE_TAPS * KT], F32R)
        DWL = sb("dw_lo", [P, PE_TAPS * KT])
        UH = [sb(f"glu_hi{s}", [P, GLU_LEN], F32R) for s in range(2)]
        UL = [sb(f"glu_lo{s}", [P, GLU_LEN], F32R) for s in range(2)]
        DGH = sb("diag_hi", [P, PE_TAPS, P], F32R)
        DGL = sb("diag_lo", [P, PE_TAPS, P], F32R)
        assert base[0] <= names["conv_act_hi"][1] + 8 * KT * T
        PR, CP = RB, TM
        base[0] = region
        OH = sb("attn_hi", [P, KT, T], F32R)
        OL = sb("attn_lo", [P, KT, T], F32R)
        KSH = sb("k_stack_hi", [P, 2, T], F32R)
        KSL = sb("k_stack_lo", [P, 2, T], F32R)
        VH = sb("v_hi", [P, BLOCKS, P], F32R)
        VL = sb("v_lo", [P, BLOCKS, P], F32R)
        QST = [sb(f"q_stack{s}", [P, 2, T], F32R) for s in range(2)]
        PH = [sb(f"probs_hi{s}", [P, 2, 2, P], F32R) for s in range(2)]
        LG = sb("logits", [P, RING, 2, 2 * P + 8])
        assert base[0] <= region_end
        base[0] = region_end
        PL = [at(f"probs_lo{s}", [P, 2, 2, P], F32R, names["relu_squared"][1] + 4 * T * s) for s in range(2)]
        NM = sb("neg_max", [P, RING, 2])
        RS = sb("prob_sum", [P, RING, 2])
        RI = sb("prob_scale", [P, RING, 2])
        RQ = sb("q_scale", [P, 2, 2 * BLOCKS])
        QZ = sb("q_square_sum", [P, 4, 2 * BLOCKS])
        assert base[0] <= nc.sbuf_usable_end
        prep = names["relu_squared"][1]
        OHOT = at("onehot", [REL_BUCKETS, P], F32, prep)
        RELB = at("rel_bias_in", [REL_BUCKETS, HEADS], F32, prep + 4 * P)
        RVT = at("bias_rows", [HEADS, RV], F32, prep + 4 * (P + HEADS))

        PS = [ctx.enter_context(nc.psum_tensor(f"bank{b}", [P, T], F32)) for b in range(8)]

        x_landed = [sem(f"x_landed{q}") for q in range(4)]
        small_landed = sem("small_landed")
        w_landed = [sem(f"w_landed{s}") for s in range(2)]
        w_hi_done = sem("w_hi_done")
        w_split = sem("w_split")
        tile_mm = sem("tile_mm")
        a_hi = sem("a_hi")
        a_lo = sem("a_lo")
        sq_done = sem("sq_done")
        ss_acc = sem("ss_acc")
        stat_mm = sem("stat_mm")
        r2_done = sem("r2_done")
        r_done = sem("r_done")
        dve_step = sem("dve_step")
        pad_done = sem("pad_done")
        glu_free = sem("glu_free")
        gate_done, u_done, tap_done = sem("gate_done"), sem("u_done"), sem("tap_done")
        uh_done, ul_done, diag_done = sem("uh_done"), sem("ul_done"), sem("diag_done")
        dw_hi, dw_lo = sem("dw_hi"), sem("dw_lo")
        prod_done, prod_added, pe_conv = sem("prod_done"), sem("prod_added"), sem("pe_conv")
        ys_acc, ln_mm, mu_done = sem("ys_acc"), sem("ln_mm"), sem("mu_done")
        yc_done, ysq_done, var_mm = sem("yc_done"), sem("ysq_done"), sem("var_mm")
        rl_inv, rl_done = sem("rl_inv"), sem("rl_done")
        yn_done, silu_done, z_hi, z_lo = sem("yn_done"), sem("silu_done"), sem("z_hi"), sem("z_lo")
        x_done = sem("x_done")
        tm_done = sem("tm_done")
        relu_done = sem("relu_done")
        hh_done, v_done, h_lo = sem("hh_done"), sem("v_done"), sem("h_lo")
        bias_mm, rows_done, rows_out, bias_in = (sem("bias_mm"), sem("rows_done"),
                                                 sem("rows_out"), sem("bias_in"))
        kv_scaled, k_biased, v_biased = (sem("kv_scaled"), sem("k_biased"),
                                                sem("v_biased"))
        k_sum_mm, k_inv, k_rstd, k_stacked = (sem("k_sum_mm"), sem("k_inv"), sem("k_rstd"),
                                              sem("k_stacked"))
        v_turned, vh_done, v_done_all = sem("v_turned"), sem("vh_done"), sem("v_split")
        q_scaled, q_biased, q_squared = (sem("q_scaled"), sem("q_biased"),
                                               sem("q_squared"))
        q_sum_mm, q_z, q_r0, q_r, q_stacked = (sem("q_sum_mm"), sem("q_z"), sem("q_r0"),
                                               sem("q_r"), sem("q_stacked"))
        s_mm, sink_in, l_done, e_done, p_done = (sem("s_mm"), sem("sink_in"), sem("l_done"),
                                                 sem("e_done"), sem("p_done"))
        ri_done, p1_done = sem("ri_done"), sem("p1_done")
        t_mm, ph_done, pl_done, pv_mm = sem("t_mm"), sem("ph_done"), sem("pl_done"), sem("pv_mm")
        o_hi, o_lo = sem("o_hi"), sem("o_lo")
        out_done = sem("out_done")
        gb_done = sem("gb_done")
        act_step = sem("act_step")

        def par(name, i=0):
            return PAR[:, COL[name] + i:COL[name] + i + 1]

        def bias_of(head, lo):
            first = BIAS[:, head, 2 * P - 1 - lo:2 * P - lo]
            return bass.AP(first.tensor, first.offset, [first.ap[0], [-1, 2 * P - lo]])

        def parx(name, i):
            return PAR[:, bass.ds(COL[name] + i, 1)]

        R_IN, R_MLP0, R_ATT, R_MLP1 = range(4)
        SMALL = 5 * 16

        block = ctx.enter_context(nc.Block())

        @block.sync
        def _(sp):
            def load_x(q):
                sp.dma_start(X[:, 2 * q:2 * q + 2, :], x_t[:, 2 * q:2 * q + 2, :]).then_inc(x_landed[q], 16)

            load_x(0)
            load_x(1)
            sp.dma_start(RAW[0][:], w_all[0]).then_inc(w_landed[0], 16)
            load_x(2)
            load_x(3)
            sp.dma_start(RAW[1][:], w_all[1]).then_inc(w_landed[1], 16)
            with sp.Fori(1, CHUNKS // 2) as i:
                for s in range(2):
                    sp.wait_ge(w_split, 2 * i + s - 1)
                    sp.dma_start(RAW[s][:], w_all[bass.ds(2 * i + s, 1)].rearrange("a p k n -> (a p) k n")).then_inc(w_landed[s], 16)
            sp.wait_ge(w_split, CHUNKS - 2)
            sp.dma_start(RAW[0][:], w_all[CHUNKS - 1]).then_inc(w_landed[0], 16)
            for t in range(KT):
                sp.wait_ge(x_done, BANK_CREDIT + 5 * KT + t + 1)
                sp.dma_start(out[:, t, :], X[:, t, :]).then_inc(out_done, 16)
            sp.wait_ge(out_done, 16 * KT)

        def hi_of_chunk(act, c, s, landed, first=False):
            act.wait_ge(w_landed[s], 16 * landed)
            if not first:
                act.wait_ge(tile_mm, 2 * (c - 1))
            act.activation(WH[s][:], RAW[s][:], ACT.Copy).then_inc(w_hi_done, 1)

        def lo_of_chunk_part(eng, c, s, part, parts):
            ks = slice(part * KT // parts, (part + 1) * KT // parts)
            eng.wait_ge(w_hi_done, c + 1)
            ins = eng.tensor_tensor(out=WL[s][:, ks, :], in0=RAW[s][:, ks, :], in1=WH[s][:, ks, :].bitcast(F32),
                                    op=ALU.subtract)
            if part == parts - 1:
                ins.then_inc(w_split, 1)

        def lo_of_chunk(eng, c, s, handover=False):
            if handover:
                eng.wait_ge(w_split, c)
            eng.wait_ge(w_hi_done, c + 1)
            eng.tensor_tensor(out=WL[s][:], in0=RAW[s][:], in1=WH[s][:].bitcast(F32),
                              op=ALU.subtract).then_inc(w_split, 1)

        def make_operand_act(act, rnd, k, j, gain):
            act.wait_ge(ss_acc, (KT + 1) * rnd + k)
            act.activation(AH[:, k, :], X[:, k, :], ACT.Identity, scale=gain).then_inc(a_hi, 1)
            act.activation(SQ[:, j, :], X[:, k, :], ACT.Square).then_inc(sq_done, 1)

        def make_operand_dve(dve, rnd, k, gain):
            dve.wait_ge(a_hi, KT * rnd + k + 1)
            dve.scalar_tensor_tensor(out=AL[:, k, :], in0=X[:, k, :], scalar=gain,
                                     in1=AH[:, k, :].bitcast(F32), op0=ALU.mult,
                                     op1=ALU.subtract).then_inc(a_lo, 1)

        def clear_sum(pool, rnd):
            if rnd:
                pool.wait_ge(stat_mm, rnd)
            pool.memset(SS[:], 0.0).then_inc(ss_acc, 1)

        def add_square(pool, rnd, k, j):
            pool.wait_ge(sq_done, KT * rnd + k + 1)
            pool.wait_ge(ss_acc, (KT + 1) * rnd + k + 1)
            pool.tensor_tensor(out=SS[:], in0=SS[:], in1=SQ[:, j, :], op=ALU.add).then_inc(ss_acc, 1)

        def product(pe, bank, s, j, k, bh, bl, start, stop):
            wh, wl = WH[s][:, k, j * P:(j + 1) * P], WL[s][:, k, j * P:(j + 1) * P]
            pe.matmul(bank, wh, bh, start=start, stop=False)
            pe.matmul(bank, wh, bl, start=False, stop=False)
            return pe.matmul(bank, wl, bh, start=False, stop=stop)

        def chunk_by_k(pe, banks, s, bh, bl, wait_k):
            for k in range(KT):
                wait_k(k)
                for j in range(2):
                    mm = product(pe, banks[j][:], s, j, k, bh[:, k, :], bl[:, k, :], k == 0, k == KT - 1)
                    if k == KT - 1:
                        mm.then_inc(tile_mm, 1)

        def statistic(pe, rnd):
            pe.wait_ge(ss_acc, (KT + 1) * (rnd + 1))
            pe.matmul(PS[7][:], ONES, SS[:], start=True, stop=True).then_inc(stat_mm, 1)

        def rstd_squared(dve, rnd):
            dve.wait_ge(stat_mm, rnd + 1)
            step(dve, dve.tensor_scalar(Z[:], PS[7][:], 1.0 / D, EPS, ALU.mult, ALU.add))
            dve.reciprocal(R2[:], Z[:]).then_inc(r2_done, 1)

        steps = {}

        def step(eng, instr, s=dve_step):
            steps[s.name] = steps.get(s.name, 0) + 1
            instr.then_inc(s, 1)
            eng.wait_ge(s, steps[s.name])

        def project_pe(pe, c0, xb, bh, bl, ready, count):
            with pe.Fori(0, 2) as i:
                for s in range(2):
                    buf = (c0 + s) % 2
                    pe.wait_ge(w_split, c0 + 2 * i + s + 1)
                    if s == 0:
                        pe.wait_ge(x_done, xb + 4 * i + 2)
                        chunk_by_k(pe, PS[0:2], buf, bh, bl, lambda k: pe.wait_ge(ready, count(k)))
                        continue
                    for j in range(2):
                        pe.wait_ge(x_done, xb + 4 * i + 2 * s + j + 1)
                        for k in range(KT):
                            mm = product(pe, PS[2 * s + j][:], buf, j, k, bh[:, k, :], bl[:, k, :],
                                         k == 0, k == KT - 1)
                        mm.then_inc(tile_mm, 1)

        def project_act(act, c0, xb, rnd, gain):
            with act.Fori(0, 2) as i:
                for s in range(2):
                    hi_of_chunk(act, c0 + 2 * i + s + 1, (c0 + s + 1) % 2, (c0 + s + 1) // 2 + i + 1)
                    for j in range(2):
                        k = 4 * i + 2 * s + j
                        act.wait_ge(x_done, BANK_CREDIT + xb + k + 1)
                        make_operand_act(act, rnd, k, j, parx(*gain(k)))

        def project_dve(dve, c0, xb, rnd, bias, gain):
            with dve.Fori(0, 2) as i:
                for s in range(2):
                    for j in range(2):
                        k = 4 * i + 2 * s + j
                        dve.wait_ge(tile_mm, 2 * c0 + k + 1)
                        dve.scalar_tensor_tensor(out=X[:, k, :], in0=PS[2 * s + j][:], scalar=parx(bias, k),
                                                 in1=X[:, k, :], op0=ALU.add, op1=ALU.add).then_inc(x_done, 1)
                        make_operand_dve(dve, rnd, k, parx(*gain(k)))

        def project_pool(pool, c0, xb, rnd):
            clear_sum(pool, rnd)
            with pool.Fori(0, 2) as i:
                for s in range(2):
                    lo_of_chunk(pool, c0 + 2 * i + s + 1, (c0 + s + 1) % 2)
                    for j in range(2):
                        add_square(pool, rnd, 4 * i + 2 * s + j, j)

        def mlp_pe(pe, l, c0, xb, rnd):
            for half in range(2):
                h0 = (2 * l + half) * HALF_TILES
                c = c0 + half * MLP_CHUNKS // 2
                with pe.Fori(0, 4) as i:
                    for s in range(2):
                        pe.wait_ge(w_split, c + 2 * i + s + 1)
                        if s == 0:
                            pe.wait_ge(relu_done, h0 + 4 * i + 2)
                            chunk_by_k(pe, PS[0:2], c0 % 2, AH, AL,
                                       lambda k: pe.wait_ge(a_lo, KT * rnd + k + 1))
                            continue
                        for j in range(2):
                            pe.wait_ge(relu_done, h0 + 4 * i + 2 * s + j + 1)
                            for k in range(KT):
                                mm = product(pe, PS[2 * s + j][:], (c0 + s) % 2, j, k, AH[:, k, :],
                                             AL[:, k, :], k == 0, k == KT - 1)
                            mm.then_inc(tile_mm, 1)
                if half == 0:
                    statistic(pe, rnd)
                c += KT
                with pe.Fori(0, 4) as i:
                    for s in range(2):
                        pe.wait_ge(w_split, c + 2 * i + s + 1)
                        for j in range(2):
                            if s == 0:
                                pe.wait_ge(x_done, BANK_CREDIT + xb + half * KT + 2 * i + j - 1)
                            for k in range(KT):
                                if j == 0:
                                    pe.wait_ge(h_lo, h0 + KT * s + k + 1)
                                mm = product(pe, PS[4 + j][:], (c0 + s) % 2, j, k, HH[:, KT * s + k, :],
                                             HL[:, KT * s + k, :], s == 0 and k == 0, s == 1 and k == KT - 1)
                            mm.then_inc(tile_mm, 1)

        def mlp_act(act, l, c0, xb, nxt):
            for half in range(2):
                h0 = (2 * l + half) * HALF_TILES
                c = c0 + half * MLP_CHUNKS // 2
                with act.Fori(0, 4) as i:
                    for s in range(2):
                        hi_of_chunk(act, c + 2 * i + s + 1, (c0 + s + 1) % 2, (c + s + 1) // 2 + i + 1)
                        for j in range(2):
                            h = 4 * i + 2 * s + j
                            act.wait_ge(tile_mm, 2 * c + h + 1)
                            act.wait_ge(v_done, h0 + h + 1)
                            act.activation(RB[:, j, :], PS[2 * s + j][:], ACT.Relu).then_inc(relu_done, 1)
                            act.wait_ge(relu_done, BANK_CREDIT + h0 + h + 1)
                            act.activation(HH[:, h, :], RB[:, j, :], ACT.Square).then_inc(hh_done, 1)
                c += KT

                def down(i, last=False):
                    for s in range(2):
                        if not (last and s == 1):
                            hi_of_chunk(act, c + 2 * i + s + 1, (c0 + s + 1) % 2, (c + s + 1) // 2 + i + 1)
                    if half == 1 and nxt is not None:
                        for j in range(2):
                            act.wait_ge(x_done, BANK_CREDIT + xb + KT + 2 * i + j + 1)
                            make_operand_act(act, nxt[0], 2 * i + j, j, parx(nxt[1], 2 * i + j))

                if half == 1 and nxt is None:
                    with act.Fori(0, 3) as i:
                        down(i)
                    down(3, last=True)
                else:
                    with act.Fori(0, 4) as i:
                        down(i)

        def mlp_dve(dve, l, c0, xb, rnd, nxt):
            for half in range(2):
                h0 = (2 * l + half) * HALF_TILES
                c = c0 + half * MLP_CHUNKS // 2
                with dve.Fori(0, 4) as i:
                    for s in range(2):
                        lo_of_chunk(dve, c + 2 * i + s + 1, (c0 + s + 1) % 2, handover=True)
                        for j in range(2):
                            h = 4 * i + 2 * s + j
                            dve.wait_ge(relu_done, BANK_CREDIT + h0 + h + 1)
                            dve.tensor_tensor(out=VB[:, j, :], in0=RB[:, j, :], in1=RB[:, j, :],
                                              op=ALU.mult).then_inc(v_done, 1)
                            dve.wait_ge(v_done, RELU_CREDIT + h0 + h + 1)
                            dve.wait_ge(hh_done, h0 + h + 1)
                            dve.tensor_tensor(out=HL[:, h, :], in0=VB[:, j, :], in1=HH[:, h, :].bitcast(F32),
                                              op=ALU.subtract).then_inc(h_lo, 1)
                if half == 0:
                    rstd_squared(dve, rnd)
                    dve.wait_ge(r2_done, rnd + 1)
                c += KT

                def down(i, last=False):
                    for s in range(2):
                        if not (last and s == 1):
                            lo_of_chunk(dve, c + 2 * i + s + 1, (c0 + s + 1) % 2)
                    for j in range(2):
                        dve.wait_ge(tile_mm, 2 * (c + 2 * i + 1) + j + 1)
                        dve.tensor_tensor(out=TM[:, j, :], in0=PS[4 + j][:], in1=R2[:],
                                          op=ALU.mult).then_inc(tm_done, 1)
                        dve.wait_ge(tm_done, (2 * l + half) * KT + 2 * i + j + 1)
                        dve.tensor_tensor(out=X[:, 2 * i + j, :], in0=X[:, 2 * i + j, :], in1=TM[:, j, :],
                                          op=ALU.add).then_inc(x_done, 1)
                        if half == 1 and nxt is not None:
                            make_operand_dve(dve, nxt[0], 2 * i + j, parx(nxt[1], 2 * i + j))

                if half == 1 and nxt is None:
                    with dve.Fori(0, 3) as i:
                        down(i)
                    down(3, last=True)
                else:
                    with dve.Fori(0, 4) as i:
                        down(i)

        STEPS = KT * BLOCKS

        def keys_from(n):
            return P if n % BLOCKS == 0 else 0

        @block.tensor
        def _(pe):
            pe.wait_ge(small_landed, SMALL)
            pe.matmul(PS[6][0:HEADS, 0:P], RELB[:], OHOT[:], start=True, stop=True).then_inc(bias_mm, 1)

            def glu_tile(m, s, j, first=False):
                if not first:
                    pe.wait_ge(glu_free, 2 * m - 2 - j)
                for k in range(KT):
                    mm = product(pe, PS[2 * s + j][:], s, j, k, AH[:, k, :], AL[:, k, :], k == 0, k == KT - 1)
                mm.then_inc(tile_mm, 1)

            def conv_taps(m, s):
                pe.wait_ge(ul_done, m + 1)
                pe.wait_ge(diag_done, m + 1)
                pe.wait_ge(tap_done, TAP_CREDIT + DVE_STEPS * (m - 1))
                for n in range(PE_TAPS):
                    tap = PE_FIRST + n
                    uh, ul = UH[s][:, tap:tap + T], UL[s][:, tap:tap + T]
                    pe.matmul(PS[4 + s][:], DGH[:, n, :], uh, start=n == 0, stop=False)
                    pe.matmul(PS[4 + s][:], DGH[:, n, :], ul, start=False, stop=False)
                    mm = pe.matmul(PS[4 + s][:], DGL[:, n, :], uh, start=False, stop=n == PE_TAPS - 1)
                mm.then_inc(pe_conv, 1)

            def glu_chunk(m, s, first=False):
                pe.wait_ge(w_split, m + 1)
                glu_tile(m, s, 1, first)
                conv_taps(m - 1, 1 - s)
                glu_tile(m, s, 0, first)

            pe.wait_ge(w_split, 1)
            chunk_by_k(pe, PS[0:2], 0, AH, AL, lambda k: pe.wait_ge(a_lo, k + 1))
            statistic(pe, R_IN)
            glu_chunk(1, 1, first=True)
            with pe.Fori(1, KT // 2) as i:
                for s in range(2):
                    glu_chunk(2 * i + s, s)
            conv_taps(KT - 1, 1)

            pe.wait_ge(ys_acc, KT + 1)
            pe.wait_ge(r2_done, 1)
            pe.matmul(PS[7][:], ONES, YS[:], start=True, stop=True).then_inc(ln_mm, 1)
            for m in range(KT):
                pe.wait_ge(ysq_done, m + 1)
                pe.matmul(PS[6][:], ONES, SQ[:, m % 2, :], start=m == 0, stop=m == KT - 1).then_inc(var_mm, 1)

            project_pe(pe, C_OUT, 0, ZH, ZL, z_lo, lambda k: k + 1)
            mlp_pe(pe, 0, C_MLP0, KT, R_MLP0)

            pe.wait_ge(w_split, C_KV + 1)
            chunk_by_k(pe, PS[6:8], C_KV % 2, AH, AL, lambda k: pe.wait_ge(a_lo, KT * R_ATT + k + 1))
            pe.wait_ge(ss_acc, (KT + 1) * (R_ATT + 1))
            pe.matmul(PS[4][:], ONES, SS[:], start=True, stop=True).then_inc(stat_mm, 1)

            def q_part(jt, ks):
                c = C_Q + jt // 2
                if 0 in ks:
                    pe.wait_ge(w_split, c + 1)
                    if jt >= 2:
                        pe.wait_ge(q_z, jt - 1)
                for k in ks:
                    mm = product(pe, PS[jt % 2][:], c % 2, jt % 2, k, AH[:, k, :], AL[:, k, :],
                                 k == 0, k == KT - 1)
                if KT - 1 in ks:
                    mm.then_inc(tile_mm, 1)

            def q_sums(jt):
                pe.wait_ge(q_squared, jt + 1)
                for n in range(BLOCKS):
                    mm = pe.matmul(PS[jt % 2][:, 2 * n:2 * n + 2], RB[:, 1, n * P:(n + 1) * P], HEAD_COLS,
                                   start=True, stop=True)
                mm.then_inc(q_sum_mm, 1)

            q_part(0, range(KT))
            pe.wait_ge(k_biased, 2)
            pe.matmul(PS[5][:], HEAD_ONES, RB[:, 1, :], start=True, stop=True).then_inc(k_sum_mm, 1)
            pe.wait_ge(v_biased, 1)
            pe.wait_ge(r2_done, R_ATT + 1)
            for n in range(BLOCKS):
                mm = pe.transpose(PS[4][:, n * P:(n + 1) * P], VB[:, 0, n * P:(n + 1) * P], IDENT)
            mm.then_inc(v_turned, 1)
            q_part(1, range(KT))

            def scores(n):
                jt, b = n // BLOCKS, n % BLOCKS
                g, lo = jt // (KT // 2), keys_from(n)
                if b == 0:
                    pe.wait_ge(q_stacked, jt + 1)
                if n == 0:
                    pe.wait_ge(k_stacked, 1)
                if n >= 2:
                    pe.wait_ge(l_done, n - 1)
                first_key = (b - 1) * P + lo
                for e in range(2):
                    q = QST[jt % 2][:, e, b * P:(b + 1) * P]
                    o = PS[2 + n % 2][:, e * 2 * P + lo:(e + 1) * 2 * P]
                    pe.matmul(o, q, KSH[:, g, first_key:(b + 1) * P], start=True, stop=False)
                    mm = pe.matmul(o, q, KSL[:, g, first_key:(b + 1) * P], start=False, stop=True)
                mm.then_inc(s_mm, 1)

            def turn(n):
                pe.wait_ge(p_done, n + 1)
                pe.wait_ge(p1_done, n + 1)
                if n >= 2:
                    pe.wait_ge(pl_done, n - 1)
                if n < 2:
                    pe.wait_ge(v_done_all, 1)
                for e in range(2):
                    for kb in range(keys_from(n) // P, 2):
                        mm = pe.transpose(PS[4 + n % 2][:, (2 * e + kb) * P:(2 * e + kb + 1) * P],
                                          LG[:, n % RING, e, kb * P:(kb + 1) * P], IDENT)
                mm.then_inc(t_mm, 1)

            def values(n):
                jt, b = n // BLOCKS, n % BLOCKS
                pe.wait_ge(pl_done, n + 1)
                if b % 2 == 0 and n >= 4:
                    pe.wait_ge(o_lo, n // 2 - 1)
                o = PS[6 + (n // 2) % 2][:, (b % 2) * 2 * P:(b % 2 + 1) * 2 * P]
                kbs = range(keys_from(n) // P, 2)
                for kb in kbs:
                    kblock = b - 1 + kb
                    ph, pl = PH[n % 2][:, :, kb, :], PL[n % 2][:, :, kb, :]
                    pe.matmul(o, VH[:, kblock, :], ph, start=kb == kbs[0], stop=False)
                    pe.matmul(o, VH[:, kblock, :], pl, start=False, stop=False)
                    mm = pe.matmul(o, VL[:, kblock, :], ph, start=False, stop=kb == 1)
                mm.then_inc(pv_mm, 1)

            q_sums(0)
            scores(0)
            scores(1)
            for n in range(STEPS + 1):
                jt, b = n // BLOCKS, n % BLOCKS
                if n + 2 < STEPS:
                    scores(n + 2)
                if jt + 2 < KT:
                    q_part(jt + 2, range(2 * b, 2 * b + 2))
                if n < STEPS:
                    turn(n)
                if n >= 1:
                    values(n - 1)
                if b == 1 and jt + 1 < KT:
                    q_sums(jt + 1)

            project_pe(pe, C_O, 3 * KT, OH, OL, o_lo, lambda k: 2 * (k + 1))
            mlp_pe(pe, 1, C_MLP1, 4 * KT, R_MLP1)

        @block.scalar
        def _(act):
            for dst, src in ((PAR, params), (CON, consts), (OHOT, onehot), (RELB, rel_bias)):
                act.dma_start(dst[:], src).then_inc(small_landed, 16)
            act.dma_start(SINK[:], sinks.broadcast_to([P, HEADS])).then_inc(small_landed, 16)
            act.wait_ge(small_landed, SMALL)
            for k in range(KT):
                act.wait_ge(x_landed[k // 2], 16)
                make_operand_act(act, R_IN, k, k % 2, par("conv_g", k))
                if k == 1:
                    hi_of_chunk(act, 0, 0, 1, first=True)

            taps = slice(COL["dw"] + PE_FIRST * KT, COL["dw"] + DVE_FIRST * KT)
            act.activation(DWH[:], PAR[:, taps], ACT.Copy).then_inc(dw_hi, 1)

            def glu(m, s, landed=None):
                act.wait_ge(pe_conv, PE_CONV_CREDIT + m)
                for n in range(PE_TAPS):
                    act.activation(DGH[:, n, :], IDENT, ACT.Identity, scale=parx("dw", (PE_FIRST + n) * KT + m))
                    ins = act.activation(DGL[:, n, :], IDENT, ACT.Identity, scale=DWL[:, bass.ds(n * KT + m, 1)])
                ins.then_inc(diag_done, 1)
                act.wait_ge(glu_free, 2 * m + 1)
                if not (isinstance(m, int) and m == 0):
                    act.wait_ge(u_done, m)
                act.activation(SG[:], TG[:], ACT.Sigmoid, bias=parx("b_in", KT + m)).then_inc(gate_done, 1)
                if landed is not None:
                    hi_of_chunk(act, m + 2, s, landed)
                conv_parts(m, s)

            def conv_parts(m, s):
                act.wait_ge(u_done, m + 1)
                act.wait_ge(pe_conv, m)
                act.activation(UH[s][:], U[s][:], ACT.Copy).then_inc(uh_done, 1)
                act.wait_ge(tap_done, TAP_CREDIT + DVE_STEPS * (m - 1))
                act.activation(CP[:, s, :], U[s][:, 0:T], ACT.Identity, scale=parx("dw", m),
                               bias=parx("dw_b", m)).then_inc(prod_done, 1)
                for n in range(1, POOL_TAPS):
                    q = (POOL_TAPS - 1) * m + n - 1
                    act.wait_ge(prod_added, q + 1)
                    act.activation(PR[:, (s * (POOL_TAPS - 1) + n - 1) % 2, :], U[s][:, n:n + T], ACT.Identity,
                                   scale=parx("dw", n * KT + m)).then_inc(prod_done, 1)

            hi_of_chunk(act, 1, 1, 1, first=True)
            act.wait_ge(r2_done, 1)
            act.activation(R[:], R2[:], ACT.Sqrt).then_inc(r_done, 1)
            act.wait_ge(dw_lo, 1)
            glu(0, 0, 2)
            with act.Fori(0, KT // 2 - 1) as i:
                for s in range(2):
                    glu(2 * i + s + 1, 1 - s, i + s + 2)
            glu(KT - 1, 1)

            act.wait_ge(ln_mm, 1)
            act.activation(MU[:], PS[7][:], ACT.Copy, scale=1.0 / D).then_inc(mu_done, 1)
            act.preload_act_table(ACT.Sqrt)
            act.wait_ge(ss_acc, KT + 1)
            for m in range(KT):
                act.wait_ge(yc_done, m + 1)
                if m >= 2:
                    act.wait_ge(var_mm, m - 1)
                act.activation(SQ[:, m % 2, :], Y[:, m, :], ACT.Square).then_inc(ysq_done, 1)
            act.wait_ge(rl_inv, 1)
            act.activation(RL[:], MU[:], ACT.Sqrt).then_inc(rl_done, 1)
            for m in range(KT):
                act.wait_ge(yn_done, m + 1)
                act.activation(Y[:, m, :], Y[:, m, :], ACT.Silu, bias=par("ln_b", m),
                               scale=par("ln_g", m)).then_inc(silu_done, 1)
                act.wait_ge(silu_done, m + 1)
                act.activation(ZH[:, m, :], Y[:, m, :], ACT.Copy).then_inc(z_hi, 1)

            project_act(act, C_OUT, 0, R_MLP0, lambda k: ("mlp_g", k))
            mlp_act(act, 0, C_MLP0, KT, (R_ATT, "attn_g"))

            for jt in range(KT):
                ins = act.activation(GB[:, jt:jt + 1], par("b_qkv", 2 + jt), ACT.Identity, scale=par("q_g"))
            ins.then_inc(gb_done, 1)
            hi_of_chunk(act, C_Q, C_Q % 2, C_Q // 2 + 1)
            act.wait_ge(r2_done, R_ATT + 1)
            act.activation(R[:], R2[:], ACT.Sqrt).then_inc(r_done, 1)
            act.wait_ge(kv_scaled, 1)
            act.activation(RB[:, 0, :], TM[:, 0, :], ACT.Identity, bias=par("b_qkv", 0)).then_inc(k_biased, 1)
            act.activation(RB[:, 1, :], TM[:, 0, :], ACT.Square, bias=par("b_qkv", 0)).then_inc(k_biased, 1)
            act.wait_ge(kv_scaled, 2)
            act.activation(VB[:, 0, :], TM[:, 1, :], ACT.Identity, bias=par("b_qkv", 1)).then_inc(v_biased, 1)
            act.wait_ge(k_inv, 1)
            act.activation(Z[:], VB[:, 1, :], ACT.Sqrt).then_inc(k_rstd, 1)
            act.preload_act_table_set("natural_log_exp_and_others")
            act.wait_ge(v_turned, 1)
            act.activation(VH[:], PS[4][:].rearrange("p (n d) -> p n d", n=BLOCKS), ACT.Copy).then_inc(vh_done, 1)
            act.wait_ge(gb_done, 1)

            def q_bias(jt):
                act.wait_ge(q_scaled, jt + 1)
                if jt:
                    act.wait_ge(q_stacked, jt)
                else:
                    act.wait_ge(k_stacked, 1)
                act.activation(RB[:, 0, :], TM[:, 0, :], ACT.Identity, bias=GB[:, jt:jt + 1],
                               scale=par("q_g")).then_inc(q_biased, 1)
                if jt:
                    act.wait_ge(q_sum_mm, jt)
                else:
                    act.wait_ge(k_sum_mm, 1)
                act.activation(RB[:, 1, :], TM[:, 0, :], ACT.Square, bias=par("b_qkv", 2 + jt)).then_inc(q_squared, 1)

            def q_rsqrt(jt):
                act.wait_ge(q_z, jt + 1)
                if jt:
                    act.wait_ge(q_r, jt)
                act.activation(QZ[:, 1, :], QZ[:, 0, :], ACT.Ln).then_inc(act_step, 1)
                act.wait_ge(act_step, jt + 1)
                act.activation(QZ[:, 2, :], QZ[:, 1, :], ACT.Exp, scale=-0.5).then_inc(q_r0, 1)

            def exps(n):
                act.wait_ge(l_done, n + 1)
                lo = keys_from(n)
                if n >= RING:
                    act.wait_ge(ri_done, n - RING + 1)
                for e in range(2):
                    row = LG[:, n % RING, e, lo:2 * P + 1]
                    ins = act.activation(row, row, ACT.Exp, bias=NM[:, n % RING, e:e + 1],
                                         accum_out=RS[:, n % RING, e:e + 1])
                ins.then_inc(e_done, 1)

            def normalise(n):
                act.wait_ge(ri_done, n + 1)
                row = LG[:, n % RING, 1, keys_from(n):2 * P]
                act.activation(row, row, ACT.Identity, scale=RI[:, n % RING, 1:2]).then_inc(p1_done, 1)

            def probs_hi(n):
                act.wait_ge(t_mm, n + 1)
                if n >= 2:
                    act.wait_ge(pv_mm, n - 1)
                kb = keys_from(n) // P
                t = PS[4 + n % 2][:].rearrange("p (e k q) -> p e k q", e=2, k=2)
                act.activation(PH[n % 2][:, :, kb:2, :], t[:, :, kb:2, :], ACT.Copy).then_inc(ph_done, 1)

            def outs_hi(p):
                act.wait_ge(pv_mm, 2 * p + 2)
                jt, half = p // 2, p % 2
                g = jt // (KT // 2)
                o = PS[6 + p % 2][g * HD:(g + 1) * HD, :].rearrange("p (n e q) -> p n e q", n=2, e=2)
                for e in range(2):
                    dst = OH[e * HD:(e + 1) * HD, jt, half * 2 * P:(half + 1) * 2 * P]
                    ins = act.activation(dst.rearrange("p (n q) -> p n q", n=2), o[:, :, e, :], ACT.Copy)
                ins.then_inc(o_hi, 1)

            q_bias(0)
            q_rsqrt(0)
            hi_of_chunk(act, C_Q + 1, (C_Q + 1) % 2, (C_Q + 1) // 2 + 1)
            exps(0)
            for n in range(STEPS + 1):
                jt, b = n // BLOCKS, n % BLOCKS
                if n < STEPS:
                    normalise(n)
                if n + 1 < STEPS:
                    exps(n + 1)
                if b == 0 and jt + 1 < KT:
                    q_bias(jt + 1)
                if n < STEPS:
                    probs_hi(n)
                if n >= 2 and n % 2 == 0:
                    outs_hi(n // 2 - 1)
                if b == 2 and jt + 1 < KT:
                    q_rsqrt(jt + 1)
                if b == 0 and jt % 2 == 0 and C_Q + jt // 2 + 2 <= C_O:
                    c = C_Q + jt // 2 + 2
                    hi_of_chunk(act, c, c % 2, c // 2 + 1)

            project_act(act, C_O, 3 * KT, R_MLP1, lambda k: ("mlp_g", KT + k))
            mlp_act(act, 1, C_MLP1, 4 * KT, None)

        @block.vector
        def _(dve):
            dve.sem_inc(x_done, BANK_CREDIT)
            dve.sem_inc(relu_done, BANK_CREDIT)
            dve.sem_inc(v_done, RELU_CREDIT)
            dve.sem_inc(gate_done, GATE_CREDIT)
            dve.sem_inc(tap_done, TAP_CREDIT)
            dve.sem_inc(pe_conv, PE_CONV_CREDIT)
            dve.sem_inc(prod_added, PRODUCT_CREDIT)
            for s in range(2):
                dve.memset(U[s][:, 0:PAD], 0.0).then_inc(pad_done, 1)
            dve.wait_ge(small_landed, SMALL)
            for k in range(KT):
                make_operand_dve(dve, R_IN, k, par("conv_g", k))
                if k == 1:
                    lo_of_chunk(dve, 0, 0)
            step(dve, dve.memset(RVT[:], NEG))
            dve.wait_ge(bias_mm, 1)
            dve.tensor_copy(RVT[:, P - 1:2 * P - 1], PS[6][0:HEADS, 0:P]).then_inc(rows_done, 1)
            rstd_squared(dve, R_IN)
            dve.wait_ge(r_done, 1)

            def scale_gate(m, s):
                dve.wait_ge(tile_mm, 2 * m + 1)
                dve.wait_ge(gate_done, GATE_CREDIT + m)
                dve.tensor_tensor(out=TG[:], in0=PS[2 * s + 1][:], in1=R[:], op=ALU.mult).then_inc(glu_free, 1)

            def scale_value(m, s):
                dve.wait_ge(tile_mm, 2 * m + 2)
                dve.tensor_tensor(out=TA[:], in0=PS[2 * s][:], in1=R[:], op=ALU.mult).then_inc(glu_free, 1)

            def glu_gate(m, s):
                dve.wait_ge(glu_free, 2 * m + 2)
                dve.wait_ge(gate_done, GATE_CREDIT + m + 1)
                if not (isinstance(m, int) and m == 0):
                    dve.wait_ge(prod_added, PRODUCT_CREDIT + (POOL_TAPS - 1) * (m - 1))
                dve.scalar_tensor_tensor(out=U[s][:, PAD:PAD + T], in0=TA[:], scalar=parx("b_in", m), in1=SG[:],
                                         op0=ALU.add, op1=ALU.mult).then_inc(u_done, 1)

            def glu_lo(m, s):
                dve.wait_ge(uh_done, m + 1)
                dve.tensor_tensor(out=UL[s][:], in0=U[s][:], in1=UH[s][:].bitcast(F32),
                                  op=ALU.subtract).then_inc(ul_done, 1)

            def conv(m, s, between):
                sums = [PS[6] if n >= POOL_SUM_AT and (n - POOL_SUM_AT) % 2 == 0 else PS[4 + s]
                        for n in range(DVE_TAPS)]
                for n, acc in enumerate(sums):
                    tap = DVE_FIRST + n
                    dst, more = acc[:], acc[:]
                    dve.wait_ge(tap_done, TAP_CREDIT + DVE_STEPS * m + n - (n == 0 or acc is not sums[n - 1]))
                    if n == 0:
                        dve.wait_ge(pe_conv, PE_CONV_CREDIT + m + 1)
                    if n == POOL_SUM_AT:
                        dve.wait_ge(prod_added, PRODUCT_CREDIT + (POOL_TAPS - 1) * (m + 1))
                        more = CP[:, s, :]
                    if n == DVE_TAPS - 1:
                        dst = Y[:, m, :]
                    dve.scalar_tensor_tensor(out=dst, in0=U[s][:, tap:tap + T], scalar=parx("dw", tap * KT + m),
                                             in1=more, op0=ALU.mult, op1=ALU.add).then_inc(tap_done, 1)
                    for f in between.get(n, ()):
                        f()
                dve.wait_ge(tap_done, TAP_CREDIT + DVE_STEPS * m + DVE_TAPS)
                dve.tensor_tensor(out=Y[:, m, :], in0=Y[:, m, :], in1=sums[-2][:], op=ALU.add).then_inc(tap_done, 1)

            def tile_step(m, s):
                conv(m - 1, 1 - s, {GATE_AFTER: [lambda: scale_gate(m, s)],
                                    VALUE_AFTER: [lambda: scale_value(m, s)],
                                    VALUE_AFTER + 1: [lambda: glu_gate(m, s)],
                                    LO_AFTER: [lambda: glu_lo(m, s)]})

            dve.wait_ge(pad_done, 2)
            scale_gate(0, 0)
            scale_value(0, 0)
            glu_gate(0, 0)
            glu_lo(0, 0)
            with dve.Fori(0, KT // 2 - 1) as i:
                for s in range(2):
                    tile_step(2 * i + s + 1, 1 - s)
            tile_step(KT - 1, 1)
            conv(KT - 1, 1, {})

            dve.wait_ge(mu_done, 1)
            dve.wait_ge(tap_done, TAP_CREDIT + DVE_STEPS * KT)
            for m in range(KT):
                dve.tensor_tensor(out=Y[:, m, :], in0=Y[:, m, :], in1=MU[:], op=ALU.subtract).then_inc(yc_done, 1)
            dve.wait_ge(var_mm, KT)
            step(dve, dve.tensor_scalar(Z[:], PS[6][:], 1.0 / D, EPS, ALU.mult, ALU.add))
            dve.wait_ge(yc_done, KT)
            dve.reciprocal(MU[:], Z[:]).then_inc(rl_inv, 1)
            dve.wait_ge(rl_done, 1)
            for n in range(KT + 2):
                if n < KT:
                    dve.tensor_tensor(out=Y[:, n, :], in0=Y[:, n, :], in1=RL[:], op=ALU.mult).then_inc(yn_done, 1)
                if n < 2:
                    continue
                m = n - 2
                dve.wait_ge(z_hi, m + 1)
                dve.tensor_tensor(out=ZL[:, m, :], in0=Y[:, m, :], in1=ZH[:, m, :].bitcast(F32),
                                  op=ALU.subtract).then_inc(z_lo, 1)

            project_dve(dve, C_OUT, 0, R_MLP0, "b_out", lambda k: ("mlp_g", k))
            mlp_dve(dve, 0, C_MLP0, KT, R_MLP0, (R_ATT, "attn_g"))

            dve.wait_ge(stat_mm, R_ATT + 1)
            step(dve, dve.tensor_scalar(Z[:], PS[4][:], 1.0 / D, EPS, ALU.mult, ALU.add))
            dve.reciprocal(R2[:], Z[:]).then_inc(r2_done, 1)
            dve.wait_ge(r_done, 2)
            for j in range(2):
                dve.wait_ge(tile_mm, 2 * C_KV + j + 1)
                dve.tensor_tensor(out=TM[:, j, :], in0=PS[6 + j][:], in1=R[:], op=ALU.mult).then_inc(kv_scaled, 1)
            dve.wait_ge(k_sum_mm, 1)
            step(dve, dve.tensor_scalar(Z[:], PS[5][:], 1.0 / HD, EPS, ALU.mult, ALU.add))
            dve.reciprocal(VB[:, 1, :], Z[:]).then_inc(k_inv, 1)
            dve.wait_ge(k_rstd, 1)
            dve.wait_ge(k_biased, 1)
            step(dve, dve.scalar_tensor_tensor(out=VB[:, 1, :], in0=RB[:, 0, :], scalar=par("k_g"), in1=Z[:],
                                               op0=ALU.mult, op1=ALU.mult))
            for g in range(2):
                src = VB[g * HD:(g + 1) * HD, 1, :]
                for h in range(2):
                    ins = dve.tensor_copy(KSH[h * HD:(h + 1) * HD, g, :], src)
            step(dve, ins)
            for g in range(2):
                src = VB[g * HD:(g + 1) * HD, 1, :]
                for h in range(2):
                    ins = dve.tensor_tensor(out=KSL[h * HD:(h + 1) * HD, g, :], in0=src,
                                            in1=KSH[g * HD:(g + 1) * HD, g, :].bitcast(F32), op=ALU.subtract)
            ins.then_inc(k_stacked, 1)
            dve.wait_ge(vh_done, 1)
            dve.tensor_tensor(out=VL[:], in0=PS[4][:].rearrange("p (n d) -> p n d", n=BLOCKS),
                              in1=VH[:].bitcast(F32), op=ALU.subtract).then_inc(v_done_all, 1)

            def q_scale(jt):
                dve.wait_ge(tile_mm, 2 * C_Q + jt + 1)
                if jt:
                    dve.wait_ge(q_squared, jt)
                else:
                    dve.wait_ge(k_biased, 2)
                dve.tensor_tensor(out=TM[:, 0, :], in0=PS[jt % 2][:], in1=R[:], op=ALU.mult).then_inc(q_scaled, 1)

            def q_square_sum(jt):
                dve.wait_ge(q_sum_mm, jt + 1)
                if jt:
                    dve.wait_ge(q_r, jt)
                dve.tensor_scalar(QZ[:, 0, :], PS[jt % 2][:, 0:2 * BLOCKS], float(HD * EPS), None,
                                  ALU.add).then_inc(q_z, 1)

            def q_stack(jt):
                dve.wait_ge(q_biased, jt + 1)
                if jt >= 2:
                    dve.wait_ge(s_mm, BLOCKS * (jt - 1))
                st = QST[jt % 2]
                dve.tensor_copy(st[0:HD, 0, :], RB[0:HD, 0, :])
                step(dve, dve.tensor_copy(st[HD:P, 1, :], RB[HD:P, 0, :]))
                dve.tensor_tensor(out=st[HD:P, 0, :], in0=RB[0:HD, 0, :], in1=st[0:HD, 0, :].bitcast(F32),
                                  op=ALU.subtract)
                dve.tensor_tensor(out=st[0:HD, 1, :], in0=RB[HD:P, 0, :], in1=st[HD:P, 1, :].bitcast(F32),
                                  op=ALU.subtract).then_inc(q_stacked, 1)

            def q_norm(jt):
                dve.wait_ge(q_r0, jt + 1)
                step(dve, dve.tensor_tensor(out=QZ[:, 3, :], in0=QZ[:, 0, :], in1=QZ[:, 2, :], op=ALU.mult))
                step(dve, dve.scalar_tensor_tensor(out=QZ[:, 3, :], in0=QZ[:, 3, :], scalar=-0.5, in1=QZ[:, 2, :],
                                                   op0=ALU.mult, op1=ALU.mult))
                dve.scalar_tensor_tensor(out=RQ[:, jt % 2, :], in0=QZ[:, 3, :], scalar=1.5, in1=QZ[:, 2, :],
                                         op0=ALU.add, op1=ALU.mult).then_inc(q_r, 1)

            def logits(n):
                jt, b, lo = n // BLOCKS, n % BLOCKS, keys_from(n)
                dve.wait_ge(s_mm, n + 1)
                dve.wait_ge(sink_in, n + 1)
                if b == 0:
                    dve.wait_ge(q_r, jt + 1)
                for e in range(2):
                    ins = dve.scalar_tensor_tensor(
                        out=LG[:, n % RING, e, lo:2 * P], in0=PS[2 + n % 2][:, e * 2 * P + lo:(e + 1) * 2 * P],
                        scalar=RQ[:, jt % 2, 2 * b + e:2 * b + e + 1], in1=bias_of(2 * jt + e, lo),
                        op0=ALU.mult, op1=ALU.add)
                step(dve, ins)
                dve.tensor_reduce(NM[:, n % RING, :], LG[:, n % RING, :, lo:2 * P + 1], AX.X, ALU.max,
                                  negate=True).then_inc(l_done, 1)

            def inverse_sum(n):
                dve.wait_ge(e_done, n + 1)
                dve.reciprocal(RI[:, n % RING, :], RS[:, n % RING, :]).then_inc(ri_done, 1)

            def probs_lo(n):
                dve.wait_ge(ph_done, n + 1)
                kb = keys_from(n) // P
                t = PS[4 + n % 2][:].rearrange("p (e k q) -> p e k q", e=2, k=2)
                dve.tensor_tensor(out=PL[n % 2][:, :, kb:2, :], in0=t[:, :, kb:2, :],
                                  in1=PH[n % 2][:, :, kb:2, :].bitcast(F32), op=ALU.subtract).then_inc(pl_done, 1)

            def outs_lo(p):
                dve.wait_ge(o_hi, p + 1)
                jt, half = p // 2, p % 2
                g = jt // (KT // 2)
                o = PS[6 + p % 2][g * HD:(g + 1) * HD, :].rearrange("p (n e q) -> p n e q", n=2, e=2)
                for e in range(2):
                    at_ = (slice(e * HD, (e + 1) * HD), jt, slice(half * 2 * P, (half + 1) * 2 * P))
                    ins = dve.tensor_tensor(out=OL[at_].rearrange("p (n q) -> p n q", n=2), in0=o[:, :, e, :],
                                            in1=OH[at_].rearrange("p (n q) -> p n q", n=2).bitcast(F32),
                                            op=ALU.subtract)
                ins.then_inc(o_lo, 1)

            q_scale(0)
            q_stack(0)
            q_square_sum(0)
            q_norm(0)
            dve.wait_ge(bias_in, 16)
            logits(0)
            for n in range(STEPS + 1):
                jt, b = n // BLOCKS, n % BLOCKS
                if b == 3 and jt + 1 < KT:
                    q_norm(jt + 1)
                if n < STEPS:
                    inverse_sum(n)
                if n + 1 < STEPS:
                    logits(n + 1)
                if b == 0 and jt + 1 < KT:
                    q_scale(jt + 1)
                if b == 1 and jt + 1 < KT:
                    q_stack(jt + 1)
                if b == 2 and jt + 1 < KT:
                    q_square_sum(jt + 1)
                if n >= 1:
                    probs_lo(n - 1)
                if n >= 3 and n % 2 == 1:
                    outs_lo((n - 3) // 2)
            outs_lo(STEPS // 2 - 1)

            project_dve(dve, C_O, 3 * KT, R_MLP1, "b_o", lambda k: ("mlp_g", KT + k))
            mlp_dve(dve, 1, C_MLP1, 4 * KT, R_MLP1, None)

        @block.gpsimd
        def _(pool):
            clear_sum(pool, R_IN)
            for k in range(KT):
                add_square(pool, R_IN, k, k % 2)
            pool.memset(YS[:], 0.0).then_inc(ys_acc, 1)
            pool.wait_ge(dw_hi, 1)
            taps = slice(COL["dw"] + PE_FIRST * KT, COL["dw"] + DVE_FIRST * KT)
            pool.tensor_tensor(out=DWL[:], in0=PAR[:, taps], in1=DWH[:].bitcast(F32),
                               op=ALU.subtract).then_inc(dw_lo, 1)
            lo_of_chunk(pool, 1, 1, handover=True)
            pool.wait_ge(rows_done, 1)
            pool.dma_start(scratch, RVT[:]).then_inc(rows_out, 16)
            pool.wait_ge(rows_out, 16)
            pool.dma_start(BIAS[:], bass.AP(scratch.tensor, 0, [[1, P], [RV, HEADS], [1, 2 * P]])
                           ).then_inc(bias_in, 16)

            def add_products(m, s):
                for n in range(1, POOL_TAPS):
                    q = (POOL_TAPS - 1) * m + n - 1
                    pool.wait_ge(prod_done, POOL_TAPS * m + n + 1)
                    pool.wait_ge(prod_added, PRODUCT_CREDIT + q)
                    pool.tensor_tensor(out=CP[:, s, :], in0=CP[:, s, :],
                                       in1=PR[:, (s * (POOL_TAPS - 1) + n - 1) % 2, :],
                                       op=ALU.add).then_inc(prod_added, 1)

            def add_channels(m):
                pool.wait_ge(tap_done, TAP_CREDIT + DVE_STEPS * (m + 1))
                pool.wait_ge(ys_acc, m + 1)
                pool.tensor_tensor(out=YS[:], in0=YS[:], in1=Y[:, m, :], op=ALU.add).then_inc(ys_acc, 1)

            for s in range(2):
                add_products(s, s)
                lo_of_chunk(pool, s + 2, s)
            with pool.Fori(0, KT // 2 - 2) as i:
                for s in range(2):
                    add_products(2 * i + s + 2, s)
                    lo_of_chunk(pool, 2 * i + s + 4, s)
                    add_channels(2 * i + s)
            add_products(KT - 2, 0)
            lo_of_chunk(pool, KT, 0)
            add_channels(KT - 4)
            add_products(KT - 1, 1)
            add_channels(KT - 3)
            add_channels(KT - 2)
            add_channels(KT - 1)

            project_pool(pool, C_OUT, 0, R_MLP0)
            clear_sum(pool, R_ATT)
            with pool.Fori(0, KT // 2) as i:
                for j in range(2):
                    add_square(pool, R_ATT, 2 * i + j, j)
            lo_of_chunk(pool, C_Q, C_Q % 2, handover=True)

            def sink(n):
                jt = n // BLOCKS
                if n >= RING:
                    pool.wait_ge(t_mm, n - RING + 1)
                pool.tensor_copy(LG[:, n % RING, :, 2 * P:2 * P + 1],
                                 SINK[:, 2 * jt:2 * jt + 2].rearrange("p (e a) -> p e a", a=1)).then_inc(sink_in, 1)

            def normalise(n):
                pool.wait_ge(ri_done, n + 1)
                row = LG[:, n % RING, 0, keys_from(n):2 * P]
                pool.tensor_scalar(row, row, RI[:, n % RING, 0:1], None, ALU.mult).then_inc(p_done, 1)

            sink(0)
            lo_of_chunk(pool, C_Q + 1, (C_Q + 1) % 2)
            sink(1)
            for n in range(STEPS):
                c, part = C_Q + 2 + n // (2 * BLOCKS), n % (2 * BLOCKS)
                normalise(n)
                if n + 2 < STEPS:
                    sink(n + 2)
                if c <= C_O and part < 4:
                    lo_of_chunk_part(pool, c, c % 2, part, 4)
            project_pool(pool, C_O, 3 * KT, R_MLP1)


def kernel(**inputs):
    import math
    import concourse.bacc as bacc
    from concourse.bass_utils import run_bass_kernel_spmd

    a = {name: np.asarray(value) for name, value in inputs.items()}

    def chunked(w, *starts):
        cols = [w[:, c:c + P].reshape(KT, P, P).transpose(1, 0, 2) for c in starts]
        return np.concatenate(cols, axis=2)

    def projection(w, first=0):
        return [chunked(w, c, c + P) for c in range(first, first + D, CHUNK)]

    def mlp(up, down):
        chunks = []
        for half in range(2):
            h = half * FF // 2
            chunks += [chunked(up, c, c + P) for c in range(h, h + FF // 2, CHUNK)]
            chunks += [chunked(down[r:r + D], c, c + P) for c in range(0, D, CHUNK)
                       for r in range(h, h + FF // 2, D)]
        return chunks

    w_in, w_qkv = a["conv_w_in"][0], a["w_qkv"][0]
    chunks = [chunked(w_in, c, D + c) for c in range(0, D, P)]
    chunks += projection(a["conv_w_out"][0])
    chunks += mlp(a["w_up"][0], a["w_down"][0])
    chunks += [chunked(w_qkv, D, D + P)] + projection(w_qkv) + projection(a["w_o"][0])
    chunks += mlp(a["w_up"][1], a["w_down"][1])
    assert len(chunks) == CHUNKS

    def rows(v):
        return v.reshape(-1, P)

    b_qkv = rows(a["b_qkv"][0])
    parts = [rows(a["conv_norm_g"][0]), rows(a["conv_b_in"][0]), rows(a["conv_dw"][0]), rows(a["conv_dw_b"][0]),
             rows(a["conv_ln_g"][0]), rows(a["conv_ln_b"][0]), rows(a["conv_b_out"][0]), rows(a["attn_norm_g"][0]),
             b_qkv[KT:], b_qkv[:KT], rows(np.tile(a["q_norm_g"][0], 2)), rows(np.tile(a["k_norm_g"][0], 2)),
             rows(a["b_o"][0]), rows(a["mlp_norm_g"])]

    head = np.arange(P) // HD
    consts = np.concatenate([np.ones((P, P)), np.eye(P), head[:, None] == head[None, :],
                             head[:, None] == np.arange(2)[None, :]], axis=1).astype(np.float32)
    dist = np.arange(P)
    exact = REL_BUCKETS // 2
    large = exact + (np.log(np.maximum(dist, 1).astype(np.float32) / exact) / math.log(REL_MAX_DIST / exact)
                     * (REL_BUCKETS - exact)).astype(np.int32)
    bucket = np.where(dist < exact, dist, np.minimum(large, REL_BUCKETS - 1))
    onehot = (np.arange(REL_BUCKETS)[:, None] == bucket[None, :]).astype(np.float32)

    arrays = {
        "w_all": np.stack(chunks),
        "x_t": np.ascontiguousarray(a["x"][0].T.reshape(KT, P, T).transpose(1, 0, 2)),
        "params": np.ascontiguousarray(np.concatenate(parts).T),
        "consts": consts,
        "onehot": onehot,
        "rel_bias": np.ascontiguousarray(a["rel_bias"]),
        "sinks": np.ascontiguousarray(a["sinks"]),
    }
    nc = bacc.Bacc("TRN2", target_bir_lowering=False, num_devices=1)
    args = [nc.dram_tensor(f"in_{n}", v.shape, mybir.dt.from_np(v.dtype), kind="ExternalInput").ap()
            for n, v in arrays.items()]
    scratch = nc.dram_tensor("bias_scratch", (HEADS, RV), F32, kind="Internal").ap()
    out = nc.dram_tensor("out_t", (P, KT, T), F32, kind="ExternalOutput").ap()
    build(nc, *args, scratch, out)
    got = run_bass_kernel_spmd(nc, [{f"in_{n}": v for n, v in arrays.items()}], core_ids=[0]).results[0]["out_t"]
    return got.transpose(1, 0, 2).reshape(D, T).T.reshape(1, T, D)
```
